# Optimizing a Trainium2 kernel written in Bass

```python
import jax, jax.numpy as jnp
from jax import lax
import numpy as np

D_MODEL = 1024
BATCH = 1
SEQ = 512
DEPTH = 2

CHUNK = 64
N_MEM = 256

SB_HEADS = 8
SB_HEAD_DIM = 64
SB_WIDTH = SB_HEADS * SB_HEAD_DIM
SB_BLOCK = 128
CV_WIDTH = D_MODEL // 2
CV_KERNEL = 31
SC_WIDTH = D_MODEL // 2
SC_KERNEL = 3
N_BRANCH = 3
OFF_SB = 0
OFF_CV = OFF_SB + 3 * SB_WIDTH
OFF_SC = OFF_CV + 2 * CV_WIDTH
OFF_GATE = OFF_SC + 3 * SC_WIDTH
IN_WIDTH = OFF_GATE + N_BRANCH * D_MODEL
XA_HEADS = 4
XA_HEAD_DIM = D_MODEL // XA_HEADS
PEER_HEADS = 8
N_KEYS = 128
N_EXPERTS = N_KEYS * N_KEYS
PEER_KEY_DIM = 128
PEER_TOPK = 16
PEER_BLOCK = 128

kernel_name = "hybrid_sb_conformer_shortconv_peer_block"

def rmsnorm(x, g, eps=1e-6):
    xf = x.astype(jnp.float32)
    y = xf * lax.rsqrt(jnp.mean(xf * xf, axis=-1, keepdims=True) + eps)
    return (y * g.astype(jnp.float32)).astype(x.dtype)

def layernorm(x, g, b, eps=1e-5):
    xf = x.astype(jnp.float32)
    mu = jnp.mean(xf, axis=-1, keepdims=True)
    var = jnp.mean(jnp.square(xf - mu), axis=-1, keepdims=True)
    y = (xf - mu) * lax.rsqrt(var + eps)
    return (y * g.astype(jnp.float32) + b.astype(jnp.float32)).astype(x.dtype)

def causal_depthwise_conv(x, w):
    k, c = w.shape
    return lax.conv_general_dilated(
        x, w[:, None, :], window_strides=(1,), padding=[(k - 1, 0)],
        dimension_numbers=("NWC", "WIO", "NWC"), feature_group_count=c)

def stick_breaking_attention(q, k, v):
    q = q.transpose(0, 2, 1, 3)
    k = k.transpose(0, 2, 1, 3)
    v = v.transpose(0, 2, 1, 3)
    seq = q.shape[2]
    scale = SB_HEAD_DIM ** -0.5
    outs = []
    for i in range(seq // SB_BLOCK):
        lo, hi = i * SB_BLOCK, (i + 1) * SB_BLOCK
        qb, kb, vb = q[:, :, lo:hi], k[:, :, :hi], v[:, :, :hi]
        z = jnp.einsum("bhqd,bhkd->bhqk", qb, kb).astype(jnp.float32) * scale
        t_pos = lo + jnp.arange(SB_BLOCK)
        s_pos = jnp.arange(hi)
        mask = s_pos[None, :] < t_pos[:, None]
        log_beta = jax.nn.log_sigmoid(z)
        log_keep = jnp.where(mask, log_beta - z, 0.0)
        after = lax.cumsum(log_keep, axis=3, reverse=True) - log_keep
        a = jnp.where(mask, jnp.exp(log_beta + after), 0.0)
        outs.append(jnp.einsum("bhqk,bhkd->bhqd", a.astype(vb.dtype), vb))
    o = jnp.concatenate(outs, axis=2)
    return o.transpose(0, 2, 1, 3)

def hybrid_mixer(xn, w_in, conv_dw_w, conv_dw_b, conv_ln_g, conv_ln_b, sc_w, w_branch, b_gate, w_out):
    bsz, seq, _ = xn.shape
    p = xn @ w_in
    qkv = p[..., OFF_SB:OFF_CV].reshape(bsz, seq, 3, SB_HEADS, SB_HEAD_DIM)
    y_sb = stick_breaking_attention(qkv[:, :, 0], qkv[:, :, 1], qkv[:, :, 2]).reshape(bsz, seq, SB_WIDTH)
    cv_val, cv_gate = jnp.split(p[..., OFF_CV:OFF_SC], 2, axis=-1)
    u = cv_val * jax.nn.sigmoid(cv_gate)
    u = causal_depthwise_conv(u, conv_dw_w) + conv_dw_b
    y_cv = jax.nn.silu(layernorm(u, conv_ln_g, conv_ln_b))
    g_b, g_c, x_in = jnp.split(p[..., OFF_SC:OFF_GATE], 3, axis=-1)
    y_sc = g_b * causal_depthwise_conv(g_c * x_in, sc_w)
    branches = jnp.stack([y_sb, y_cv, y_sc], axis=2)
    proj = jnp.einsum("bsnc,ncd->bsnd", branches, w_branch)
    gates = jax.nn.sigmoid((p[..., OFF_GATE:] + b_gate).reshape(bsz, seq, N_BRANCH, D_MODEL))
    merged = jnp.sum(gates * proj, axis=2)
    return merged @ w_out

def memory_cross_attention(hn, mem, g_mem, wq, wkv, wo):
    bsz, seq, _ = hn.shape
    n_mem = mem.shape[1]
    q = (hn @ wq).reshape(bsz, seq, XA_HEADS, XA_HEAD_DIM)
    kv = (rmsnorm(mem, g_mem) @ wkv).reshape(bsz, n_mem, 2, XA_HEADS, XA_HEAD_DIM)
    k, v = kv[:, :, 0], kv[:, :, 1]
    s = jnp.einsum("bshd,bmhd->bhsm", q, k).astype(jnp.float32) * (XA_HEAD_DIM ** -0.5)
    a = jax.nn.softmax(s, axis=-1).astype(v.dtype)
    o = jnp.einsum("bhsm,bmhd->bshd", a, v).reshape(bsz, seq, D_MODEL)
    return o @ wo

def peer_ffn(hn, wq, sub_keys, u, v):
    bsz, seq, d = hn.shape
    q = (hn @ wq).reshape(bsz, seq, PEER_HEADS, 2, PEER_KEY_DIM)
    sc = jnp.einsum("bshpc,hpnc->bshpn", q, sub_keys).astype(jnp.float32)
    v1, i1 = lax.top_k(sc[..., 0, :], PEER_TOPK)
    v2, i2 = lax.top_k(sc[..., 1, :], PEER_TOPK)
    cand = (v1[..., :, None] + v2[..., None, :]).reshape(bsz, seq, PEER_HEADS, PEER_TOPK * PEER_TOPK)
    top, ci = lax.top_k(cand, PEER_TOPK)
    e1 = jnp.take_along_axis(i1, ci // PEER_TOPK, axis=-1)
    e2 = jnp.take_along_axis(i2, ci % PEER_TOPK, axis=-1)
    idx = e1 * N_KEYS + e2
    g = jax.nn.softmax(top, axis=-1).astype(hn.dtype)
    n_tok = bsz * seq
    n_sel = PEER_HEADS * PEER_TOPK
    xt = hn.reshape(n_tok // PEER_BLOCK, PEER_BLOCK, d)
    it = idx.reshape(n_tok // PEER_BLOCK, PEER_BLOCK, n_sel)
    gt = g.reshape(n_tok // PEER_BLOCK, PEER_BLOCK, n_sel)

    def block(args):
        xb, ib, gb = args
        a = jnp.einsum("td,ted->te", xb, u[ib])
        w = gb * jax.nn.gelu(a, approximate=False)
        return jnp.einsum("te,ted->td", w, v[ib])

    return lax.map(block, (xt, it, gt)).reshape(bsz, seq, d)

def setup_inputs(seed: int = 0) -> dict:
    key = jax.random.key(seed)
    ks = jax.random.split(key, 24)
    f32 = jnp.float32
    nrm = lambda k, shape, s: jax.random.normal(k, shape, f32) * s
    gain = lambda k, shape: 1.0 + 0.01 * jax.random.normal(k, shape, f32)
    L, D = DEPTH, D_MODEL
    return {
        "x": jax.random.normal(ks[0], (BATCH, SEQ, D), f32),
        "mem": jax.random.normal(ks[1], (BATCH, N_MEM, D), f32),
        "norm_mix_g": gain(ks[2], (L, D)),
        "w_in": nrm(ks[3], (L, D, IN_WIDTH), D ** -0.5),
        "conv_dw_w": nrm(ks[4], (L, CV_KERNEL, CV_WIDTH), CV_KERNEL ** -0.5),
        "conv_dw_b": nrm(ks[5], (L, CV_WIDTH), 0.01),
        "conv_ln_g": gain(ks[6], (L, CV_WIDTH)),
        "conv_ln_b": nrm(ks[7], (L, CV_WIDTH), 0.01),
        "sc_w": nrm(ks[8], (L, SC_KERNEL, SC_WIDTH), SC_KERNEL ** -0.5),
        "w_branch": nrm(ks[9], (L, N_BRANCH, SB_WIDTH, D), SB_WIDTH ** -0.5),
        "b_gate": nrm(ks[10], (L, N_BRANCH * D), 0.01),
        "w_out": nrm(ks[11], (L, D, D), D ** -0.5),
        "norm_xa_g": gain(ks[12], (L, D)),
        "norm_mem_g": gain(ks[13], (L, D)),
        "xa_wq": nrm(ks[14], (L, D, D), D ** -0.5),
        "xa_wkv": nrm(ks[15], (L, D, 2 * D), D ** -0.5),
        "xa_wo": nrm(ks[16], (L, D, D), D ** -0.5),
        "norm_ffn_g": gain(ks[17], (L, D)),
        "peer_wq": nrm(ks[18], (L, D, PEER_HEADS * 2 * PEER_KEY_DIM), D ** -0.5),
        "peer_keys": nrm(ks[19], (L, PEER_HEADS, 2, N_KEYS, PEER_KEY_DIM), PEER_KEY_DIM ** -0.5),
        "peer_u": nrm(ks[20], (L, N_EXPERTS, D), D ** -0.5),
        "peer_v": nrm(ks[21], (L, N_EXPERTS, D), PEER_HEADS ** -0.5),
        "final_g": gain(ks[22], (D,)),
    }

def reference(x, mem, norm_mix_g, w_in, conv_dw_w, conv_dw_b, conv_ln_g, conv_ln_b, sc_w,
              w_branch, b_gate, w_out, norm_xa_g, norm_mem_g, xa_wq, xa_wkv, xa_wo,
              norm_ffn_g, peer_wq, peer_keys, peer_u, peer_v, final_g):
    h = x
    for l in range(DEPTH):
        h = h + hybrid_mixer(rmsnorm(h, norm_mix_g[l]), w_in[l], conv_dw_w[l], conv_dw_b[l],
                             conv_ln_g[l], conv_ln_b[l], sc_w[l], w_branch[l], b_gate[l], w_out[l])
        h = h + memory_cross_attention(rmsnorm(h, norm_xa_g[l]), mem, norm_mem_g[l],
                                       xa_wq[l], xa_wkv[l], xa_wo[l])
        h = h + peer_ffn(rmsnorm(h, norm_ffn_g[l]), peer_wq[l], peer_keys[l], peer_u[l], peer_v[l])
    return rmsnorm(h, final_g)


_drawn_inputs = setup_inputs


def setup_inputs(seed=0):
    import zlib

    import numpy as np

    out = dict(_drawn_inputs(seed))
    spreads = {}
    factors = {'conv_ln_g': 3.082,
     'conv_ln_b': 3.306,
     'b_gate': 3.616,
     'norm_xa_g': 5.547,
     'norm_mem_g': 4.755,
     'final_g': 31.926,
     'norm_ffn_g': 3.615}
    for name, (base, spread) in spreads.items():
        noise = np.random.default_rng([zlib.crc32(name.encode()), seed]).standard_normal(out[name].shape)
        drawn = base * np.exp(spread * noise) if base else spread * noise
        out[name] = __import__('jax').numpy.asarray(drawn.astype(out[name].dtype))
    for name, factor in factors.items():
        out[name] = (out[name] * factor).astype(out[name].dtype)
    return out
```

```python
from contextlib import ExitStack

import concourse.bass as bass
from concourse import mybir

P = 128
T = 512
D = 1024
KC = D // P
LAYERS = 2
TB = T // P
N_MEM = 256
MB = N_MEM // P
SB_TILES = 4
SB_HEADS = 8
CV_TAPS = 31
SC_TAPS = 3
XA_HEADS = 4
XA_DH = D // XA_HEADS
PH = 8
LISTS = 2 * PH
NK = 128
TOPK = 16
SEL = PH * TOPK
NEG = -3.0e38

PAR, PAR_COLS = {}, 0
for _n, _c in (("mix_g", KC), ("xa_g", KC), ("mem_g", KC), ("ffn_g", KC), ("cw", SB_TILES * CV_TAPS),
               ("cb", SB_TILES), ("lng", SB_TILES), ("lnb", SB_TILES), ("scw", SB_TILES * SC_TAPS),
               ("bg", 3 * KC), ("fin_g", KC)):
    PAR[_n] = PAR_COLS
    PAR_COLS += _c

FRONT = 12 + 8 + 12
BACK = 8 + 16 + 8 + 8 + 16
GATES = 3 * KC
PAIRS = NK // 2
FIRST = FRONT // 4 + KC + BACK // 4
SLOT_USES = FIRST + PAIRS
HROWS = 8
ROUNDS = 2 * KC

F32 = mybir.dt.float32
F32R = mybir.dt.float32r
BF16 = mybir.dt.bfloat16
U32 = mybir.dt.uint32
ACT = mybir.ActivationFunctionType
ALU = mybir.AluOpType
AX = mybir.AxisListType

ZW = [T - P * sb for sb in range(TB)]
ZO = [0, 512, 1024, 896]
ZCOLS = sum(ZW)
CONSTS = ("ident", "ones", "negones", "tri", "iota", "negmask", "iota16")


def build_trunk(nc, xT, memT, par_d, const_d, front_d, gates_d, branch_d, back_d, keys_d, u_d, v_d, outT):
    gate_d = nc.dram_tensor("gate_table", (NK, P, T), F32, kind="Internal").ap()
    ctx = ExitStack()
    with ctx:
        def sem(name):
            return ctx.enter_context(nc.semaphore(name))

        top = [(nc.sbuf_base + 63) // 64 * 64]

        def region(size):
            at = top[0]
            top[0] += (size + 31) // 32 * 32
            return at

        def place(name, at, shape, dt):
            return nc.alloc_sbuf_tensor_at(name, [P] + list(shape), dt, offset=at)

        SLOT = [0, 1024, 2048, 3072]
        RING = 3 * 1024 + 1536
        raw = place("raw", region(RING * 4), [RING], F32)
        whi = place("whi", region(RING * 4), [RING], F32R)
        wlo = place("wlo", region(RING * 4), [RING], F32R)
        h = place("h", region(KC * T * 4), [KC, T], F32)
        xhi = place("xhi", region(KC * T * 4), [KC, T], F32R)
        xlo = place("xlo", region(KC * T * 4), [KC, T], F32R)
        E = region(24 * T * 4)
        bhi = place("bhi", E, [12, T], F32R)
        blo = place("blo", E + 12 * T * 4, [12, T], F32R)
        sp = place("sp", E + 4 * T * 4, [ZCOLS], F32)
        soft = place("soft", E + 16 * T * 4, [ZCOLS], F32)
        mem = place("mem", E, [KC, N_MEM], F32)
        mhi = place("mhi", E + 8192, [KC, N_MEM], F32R)
        mlo = place("mlo", E + 16384, [KC, N_MEM], F32R)
        xvT = place("xvT", E + 24576, [KC, N_MEM], F32)
        xkT = place("xkT", E + 32768, [KC, N_MEM], F32)
        xv = place("xv", E + 40960, [MB, D], F32)
        ohi = place("ohi", E, [KC, T], F32R)
        olo = place("olo", E + 16384, [KC, T], F32R)
        F = region(16 * T * 4)
        qT = place("qT", F, [SB_TILES, T], F32)
        kT = place("kT", F + 8192, [SB_TILES, T], F32)
        vT = place("vT", F + 16384, [SB_TILES, T], F32)
        conv = place("conv", F + 16384, [SB_TILES, T], F32)
        vtok = place("vtok", F + 24576, [TB, T], F32)
        sc_c = place("sc_c", F, [T], F32)
        sc_o = place("sc_o", F + 2048, [T], F32)
        yt = place("yt", F + 8192, [2, T], F32)
        mghi = place("mghi", F, [KC, T], F32R)
        mglo = place("mglo", F + 16384, [KC, T], F32R)
        xqT = place("xqT", F, [KC, T], F32)
        prob = place("prob", F + 16384, [2, TB * N_MEM], F32)
        probT = place("probT", F + 24576, [MB, T], F32)
        gbuf = place("gbuf", E, [NK, P], F32)
        keys = place("keys", E + 65536, [LISTS, NK], F32)
        onehot2 = place("onehot2", E + 65536, [HROWS, NK], F32)
        S = E + 65536 + 4096
        picks = place("picks", S, [SEL], F32)
        pick_i = place("pick_i", S + 512, [SEL], U32)
        rank = place("rank", S + 1024, [2, SEL], U32)
        eidx = place("eidx", S + 2048, [3, SEL], F32)
        vals = place("vals", E + 65536 + 8192, [TB, LISTS, TOPK], F32)
        inds = place("inds", E + 65536 + 12288, [TB, LISTS, TOPK], U32)
        act_e = place("act_e", E, [2, T], F32)
        gtile = place("gtile", E + 4096, [2, 2, T], F32)
        eh = place("eh", E + 12288, [2, 2, T], F32R)
        el = place("el", E + 20480, [2, 2, T], F32R)
        weighted = place("weighted", E + 28672, [2, T], F32)
        const = place("const", region(6 * 512 + 64), [6 * P + TOPK], F32)
        identb = place("identb", region(256), [P], BF16)
        negmaskb = place("negmaskb", region(256), [P], BF16)
        par = place("par", region(PAR_COLS * 4), [PAR_COLS], F32)
        std = place("std", region(T * 4), [T], F32)
        SQ = region(4 * T * 4)
        sq = place("sq", SQ, [2, T], F32)
        xf = place("xf", SQ + 2 * T * 4, [2, T], F32)
        sg = place("sg", SQ, [3, T], F32)
        pqT = place("pqT", SQ, [2, T], F32)
        rest = place("rest", SQ + 2 * T * 4, [TB, NK], F32)
        cand = place("cand", SQ, [PH, TOPK * TOPK], F32)
        UP = region(SB_TILES * (T + 30) * 4 + (T + 2) * 4)
        upad = place("upad", UP, [SB_TILES, T + 30], F32)
        cpad = place("cpad", UP + SB_TILES * (T + 30) * 4, [T + 2], F32)
        lookup = place("lookup", UP, [SEL, TOPK], F32)
        selT = place("selT", SQ + HROWS * NK * 4, [3, P], F32)
        small = place("small", region(64 * 4), [64], F32)
        assert top[0] <= nc.sbuf_usable_end, (top[0], nc.sbuf_usable_end)
        onehot1 = place("onehot1", SQ, [HROWS, NK], F32)

        ps = ctx.enter_context(nc.psum_tensor("ps", [P, 8, T], F32))

        def cst(name, w=P):
            k = CONSTS.index(name) * P
            return const[:, k:k + w]

        def pc(name, k):
            k += PAR[name]
            return par[:, k:k + 1]

        loaded = [sem(f"loaded{s}") for s in range(4)]
        split = [sem(f"split{s}") for s in range(4)]
        used = [sem(f"used{s}") for s in range(4)]
        x_loaded, par_loaded, const_loaded, mem_loaded, keys_loaded = (
            sem(n) for n in ("x_loaded", "par_loaded", "const_loaded", "mem_loaded", "keys_loaded"))
        consts_ready = sem("consts_ready")
        sq_ready, sq_used, std_ready, xf_ready, xhi_ready, xlo_ready = (
            sem(n) for n in ("sq_ready", "sq_used", "std_ready", "xf_ready", "xhi_ready", "xlo_ready"))
        h_ready = sem("h_ready")
        qkv_copied, vt_done, vt_copied = sem("qkv_copied"), sem("vt_done"), sem("vt_copied")
        z_done, ln_ready, sp_ready, c_done, a_ready, y_done = (
            sem(n) for n in ("z_done", "ln_ready", "sp_ready", "c_done", "a_ready", "y_done"))
        yhi_ready, ylo_ready = sem("yhi_ready"), sem("ylo_ready")
        cv_sig, cv_u, conv_ready = sem("cv_sig"), sem("cv_u"), sem("conv_ready")
        mu_done, dev_ready, dsq_ready, var_done, ln_std, ln_scaled, chi_ready, clo_ready = (
            sem(n) for n in ("mu_done", "dev_ready", "dsq_ready", "var_done", "ln_std", "ln_scaled", "chi_ready", "clo_ready"))
        sc_copied, sc_cx, sc_y, shi_ready, slo_ready = (
            sem(n) for n in ("sc_copied", "sc_cx", "sc_y", "shi_ready", "slo_ready"))
        gate_sig, br_done, br_used, mlo_ready = (sem(n) for n in ("gate_sig", "br_done", "br_used", "mlo_ready"))
        kv_copied, xvt_done, xvt_copied, xq_copied = (sem(n) for n in ("kv_copied", "xvt_done", "xvt_copied", "xq_copied"))
        xs_done, xs_neg, xs_exp, xs_norm, xt_done, xt_copied, xo_done, xohi_ready, xolo_ready = (
            sem(n) for n in ("xs_done", "xs_neg", "xs_exp", "xs_norm", "xt_done", "xt_copied", "xo_done", "xohi_ready", "xolo_ready"))
        pq_copied, score_done, score_used, top_ready = (sem(n) for n in ("pq_copied", "score_done", "score_used", "top_ready"))
        pick_diff, pick_exp, pick_ready, selT_done, selT_ready = (
            sem(n) for n in ("pick_diff", "pick_exp", "pick_ready", "selT_done", "selT_ready"))
        rows_ready, rows_free, g_copied, g_stored = (sem(n) for n in ("rows_ready", "rows_free", "g_copied", "g_stored"))
        gelu_ready, w_ready, eh_ready, el_ready, v_done, acc_done = (
            sem(n) for n in ("gelu_ready", "w_ready", "eh_ready", "el_ready", "v_done", "acc_done"))
        gt_loaded = [sem(f"gt_loaded{k}") for k in range(2)]
        out_ready, out_stored = sem("out_ready"), sem("out_stored")

        block = ctx.enter_context(nc.Block())
        NORMS = 4 * KC
        ACC = PAIRS * KC
        zps = ps[:, 4:7, :].rearrange("p a b -> p (a b)")

        @block.sync
        def _(sp_):
            eng = sp_
            eng.dma_start(h[:, :, :], xT).then_inc(x_loaded, 16)
            eng.dma_start(const[:, :], const_d).then_inc(const_loaded, 16)

            def feed(s, L, use, row, src, width=1024):
                at = eng.snap(row)
                n = eng.snap(L * SLOT_USES + use)
                eng.wait_ge(split[s], n)
                eng.dma_start(raw[:, SLOT[s]:SLOT[s] + width], src[at]).then_inc(loaded[s], 16)

            with eng.Fori(0, LAYERS) as L:
                lay = eng.snap(L * 1)
                eng.wait_ge(acc_done, L * ACC)
                eng.dma_start(par[:, :], par_d[lay]).then_inc(par_loaded, 16)
                with eng.Fori(0, FRONT // 4) as i:
                    for s in range(4):
                        feed(s, L, i, L * FRONT + i * 4 + s, front_d)
                with eng.Fori(0, KC) as i:
                    for s in range(3):
                        feed(s, L, i + FRONT // 4, L * GATES + i * 3 + s, gates_d)
                    feed(3, L, i + FRONT // 4, L * KC + i, branch_d, 1536)
                eng.wait_ge(used[3], L * FIRST + (FRONT // 4 + KC))
                eng.dma_start(mem[:, :, :], memT).then_inc(mem_loaded, 16)
                XB = (BACK - LISTS) // 4
                with eng.Fori(0, XB) as i:
                    for s in range(4):
                        feed(s, L, i + FRONT // 4 + KC, L * BACK + i * 4 + s, back_d)
                lay = eng.snap(L * 1)
                eng.wait_ge(h_ready, (L + 1) * ROUNDS)
                eng.dma_start(keys[:, :, :], keys_d[lay]).then_inc(keys_loaded, 16)
                with eng.Fori(0, LISTS // 4) as i:
                    for s in range(4):
                        feed(s, L, i + (FRONT // 4 + KC + XB), L * BACK + i * 4 + (s + BACK - LISTS), back_d)
                for s in range(2):
                    feed(s, L, FIRST, L * NK + s, u_d)
                with eng.Fori(0, TB) as b:
                    col = eng.snap(b * P)
                    eng.wait_ge(g_copied, (L * TB + b + 1) * (P // 4))
                    eng.dma_start(gate_d[:, :, bass.ds(col, P)].rearrange("a p t -> p a t"),
                                  gbuf[:, :, :]).then_inc(g_stored, 16)
                eng.wait_ge(g_stored, (L + 1) * (16 * TB))

                def feed_gates(k, pair):
                    at = eng.snap(pair * 2)
                    eng.dma_start(gtile[:, k, :, :], gate_d[bass.ds(at, 2)].rearrange("a p t -> p a t")).then_inc(gt_loaded[k], 16)

                feed_gates(0, L * 0)
                feed_gates(1, L * 0 + 1)
                with eng.Fori(0, PAIRS // 2 - 1) as j:
                    for k in range(2):
                        for s in range(2):
                            feed(s, L, j * 2 + (FIRST + 1 + k), L * NK + j * 4 + (2 * k + 2 + s), u_d)
                        for s in range(2):
                            feed(2 + s, L, j * 2 + (FIRST + k), L * NK + j * 4 + (2 * k + s), v_d)
                        at = eng.snap(j * 4 + (2 * k + 4))
                        eng.wait_ge(w_ready, L * NK + j * 4 + (2 * k + 2))
                        eng.dma_start(gtile[:, k, :, :], gate_d[bass.ds(at, 2)].rearrange("a p t -> p a t")).then_inc(gt_loaded[k], 16)
                for s in range(2):
                    feed(s, L, FIRST + PAIRS - 1, L * NK + (NK - 2 + s), u_d)
                for k in range(2):
                    for s in range(2):
                        feed(2 + s, L, FIRST + PAIRS - 2 + k, L * NK + (NK - 4 + 2 * k + s), v_d)
            eng.wait_ge(out_ready, KC)
            eng.dma_start(outT, h[:, :, :]).then_inc(out_stored, 16)
            eng.wait_ge(out_stored, 16)

        @block.gpsimd
        def _(pool):
            eng = nc.gpsimd

            def cut(s, L, use, free=None, width=1024):
                a, b = SLOT[s], SLOT[s] + width
                pool.wait_ge(loaded[s], (L * SLOT_USES + use + 1) * 16)
                if free is None:
                    pool.wait_ge(used[s], L * (SLOT_USES if s < 2 else FIRST) + use)
                else:
                    pool.wait_ge(v_done, free)
                pool.nop(nofuse=True)
                eng.tensor_copy(whi[:, a:b], raw[:, a:b])
                pool.drain()
                eng.tensor_tensor(wlo[:, a:b], raw[:, a:b], whi[:, a:b].bitcast(F32), ALU.subtract).then_inc(split[s], 1)

            with pool.Fori(0, LAYERS) as L:
                pool.wait_ge(v_done, L * ACC)
                pool.nop(nofuse=True)
                with pool.Fori(0, FRONT // 4) as i:
                    for s in range(4):
                        cut(s, L, i)
                with pool.Fori(FRONT // 4, FRONT // 4 + KC) as i:
                    for s in range(3):
                        cut(s, L, i)
                    cut(3, L, i, width=1536)
                with pool.Fori(FRONT // 4 + KC, FIRST) as i:
                    for s in range(4):
                        cut(s, L, i)
                for s in range(2):
                    cut(s, L, FIRST)
                for s in range(2):
                    pool.wait_ge(used[2 + s], (L + 1) * FIRST)
                    pool.nop(nofuse=True)
                with pool.Fori(0, PAIRS - 1) as n:
                    for s in range(2):
                        cut(s, L, n + (FIRST + 1))
                    for s in range(2):
                        cut(2 + s, L, n + FIRST, free=L * ACC + n * KC)
                for s in range(2):
                    cut(2 + s, L, FIRST + PAIRS - 1, free=L * ACC + (PAIRS - 1) * KC)

        @block.scalar
        def _(act):
            A = nc.scalar.activation
            eps6, eps5 = small[:, 0:1], small[:, 1:2]

            def panel(s, L, use):
                act.wait_ge(used[s], L * (SLOT_USES if s < 2 else FIRST) + use + 1)

            def norm(L, k, src, w, hi):
                for c in range(KC):
                    n = k * KC + c
                    act.wait_ge(sq_used, L * NORMS + (n - 1 if n >= 2 else 0))
                    A(sq[:, c % 2, 0:w], src(c), ACT.Square).then_inc(sq_ready, 1)
                act.wait_ge(sq_used, L * NORMS + (k + 1) * KC)
                A(std[:, 0:w], ps[:, 7, 0:w], ACT.Sqrt, scale=1.0 / D, bias=eps6).then_inc(std_ready, 1)
                for c in range(KC if hi is not None else 0):
                    act.wait_ge(xf_ready, L * NORMS + k * KC + c + 1)
                    A(hi[:, c, :], xf[:, c % 2, 0:w], ACT.Copy).then_inc(xhi_ready, 1)

            act.wait_ge(consts_ready, 4)
            act.wait_ge(x_loaded, 16)
            with act.Fori(0, LAYERS) as L:
                act.wait_ge(par_loaded, (L + 1) * 16)
                act.wait_ge(acc_done, L * ACC)
                norm(L, 0, lambda c: h[:, c, :], T, xhi)
                for i in range(12):
                    panel(i % 4, L, i // 4)
                    A((qT, kT, vT)[i // 4][:, i % 4, :], ps[:, i % 4, :], ACT.Copy, scale=0.125 if i < 4 else 1.0).then_inc(qkv_copied, 1)
                for b in range(TB):
                    act.wait_ge(vt_done, L * TB + b + 1)
                    A(vtok[:, b, :], ps[:, 4 + b, :], ACT.Copy).then_inc(vt_copied, 1)

                def cv(ct):
                    n = 2 * ct + 1
                    panel(n % 4, L, 3 + n // 4)
                    act.wait_ge(cv_u, L * SB_TILES + max(0, ct - 1))
                    A(xf[:, ct % 2, :], ps[:, n % 4, :], ACT.Sigmoid).then_inc(cv_sig, 1)

                def sc_copy(ct):
                    n = 8 + 3 * ct + 1
                    panel(n % 4, L, 3 + n // 4)
                    act.wait_ge(sc_cx, L * SB_TILES + ct)
                    A(sc_c[:, :], ps[:, n % 4, :], ACT.Copy).then_inc(sc_copied, 1)

                def sc_hi(ct):
                    act.wait_ge(sc_y, L * SB_TILES + ct + 1)
                    A(bhi[:, 8 + ct, :], yt[:, ct % 2, :], ACT.Copy).then_inc(shi_ready, 1)

                for hd in range(SB_HEADS):
                    n = L * SB_HEADS + hd + 1
                    act.wait_ge(z_done, n)
                    A(soft[:, :], zps[:, 0:ZCOLS], ACT.Abs)
                    act.drain()
                    A(soft[:, :], soft[:, :], ACT.Exp, scale=-1.0)
                    act.drain()
                    A(soft[:, :], soft[:, :], ACT.Ln, bias=1.0).then_inc(ln_ready, 1)
                    act.wait_ge(c_done, n)
                    A(soft[:, :], zps[:, 0:ZCOLS], ACT.Exp).then_inc(a_ready, 1)
                    if hd < 4:
                        cv(hd)
                    if hd >= 5:
                        sc_copy(hd - 5)
                    if hd >= 6:
                        sc_hi(hd - 6)
                    if hd % 2:
                        act.wait_ge(y_done, n)
                        A(bhi[:, hd // 2, :], ps[:, 7, :], ACT.Copy).then_inc(yhi_ready, 1)
                sc_hi(2)
                sc_copy(3)
                sc_hi(3)
                for ct in range(SB_TILES):
                    act.wait_ge(dev_ready, L * SB_TILES + ct + 1)
                    if ct >= 2:
                        act.wait_ge(var_done, L * SB_TILES + ct - 1)
                    A(sq[:, ct % 2, :], conv[:, ct, :], ACT.Square).then_inc(dsq_ready, 1)
                act.wait_ge(var_done, (L + 1) * SB_TILES)
                A(std[:, :], ps[:, 7, :], ACT.Sqrt, scale=1.0 / (SB_TILES * P), bias=eps5).then_inc(ln_std, 1)
                for ct in range(SB_TILES):
                    act.wait_ge(ln_scaled, L * SB_TILES + ct + 1)
                    A(conv[:, ct, :], conv[:, ct, :], ACT.Silu, scale=pc("lng", ct), bias=pc("lnb", ct))
                    act.drain()
                    A(bhi[:, 4 + ct, :], conv[:, ct, :], ACT.Copy).then_inc(chi_ready, 1)
                for dt in range(KC):
                    act.wait_ge(mlo_ready, L * KC + dt)
                    for b in range(3):
                        panel(b, L, FRONT // 4 + dt)
                        A(sg[:, b, :], ps[:, b, :], ACT.Sigmoid, bias=pc("bg", b * KC + dt)).then_inc(gate_sig, 1)
                act.wait_ge(mlo_ready, (L + 1) * KC)
                act.wait_ge(mem_loaded, (L + 1) * 16)
                norm(L, 1, lambda c: mem[:, c, :], N_MEM, mhi)
                act.wait_ge(h_ready, L * ROUNDS + KC)
                norm(L, 2, lambda c: h[:, c, :], T, xhi)
                base = FRONT // 4 + KC + 2
                for i in range(16):
                    panel(i % 4, L, base + i // 4)
                    A((xkT if i < 8 else xvT)[:, i % 8, :], ps[:, i % 4, 0:N_MEM], ACT.Copy).then_inc(kv_copied, 1)
                for m in range(MB):
                    act.wait_ge(xvt_done, L * MB + m + 1)
                    A(xv[:, m, :], ps[:, 4 + 2 * m:6 + 2 * m, :].rearrange("p a b -> p (a b)"), ACT.Copy).then_inc(xvt_copied, 1)
                for i in range(8):
                    panel(i % 4, L, base + 4 + i // 4)
                    A(xqT[:, i, :], ps[:, i % 4, :], ACT.Copy, scale=XA_DH ** -0.5).then_inc(xq_copied, 1)
                for hd in range(XA_HEADS):
                    act.wait_ge(xs_neg, L * XA_HEADS + hd + 1)
                    for tb in range(TB):
                        a = 8 + 4 * (hd % 2) + tb
                        A(prob[:, hd % 2, tb * N_MEM:(tb + 1) * N_MEM],
                          ps[:, 2 * (hd % 2) + tb // 2, (tb % 2) * N_MEM:(tb % 2 + 1) * N_MEM],
                          ACT.Exp, bias=small[:, a:a + 1], accum_out=small[:, a + 8:a + 9]).then_inc(xs_exp, 1)
                    act.wait_ge(xo_done, L * (XA_HEADS * 2) + hd * 2)
                    for m in range(MB):
                        act.wait_ge(xt_done, L * (XA_HEADS * MB) + hd * MB + m + 1)
                        A(probT[:, m, :], ps[:, 4 + m, :], ACT.Copy).then_inc(xt_copied, 1)
                    for c in range(2):
                        act.wait_ge(xo_done, L * (XA_HEADS * 2) + hd * 2 + c + 1)
                        A(ohi[:, 2 * hd + c, :], ps[:, 6 + c, :], ACT.Copy).then_inc(xohi_ready, 1)
                act.wait_ge(h_ready, (L + 1) * ROUNDS)
                norm(L, 3, lambda c: h[:, c, :], T, xhi)
                for l in range(LISTS):
                    panel(l % 4, L, base + 8 + l // 4)
                    if l >= 2:
                        act.wait_ge(score_done, L * LISTS + l - 1)
                    A(pqT[:, l % 2, :], ps[:, l % 4, :], ACT.Copy).then_inc(pq_copied, 1)
                with act.Fori(0, TB) as b:
                    act.wait_ge(pick_diff, L * TB + b + 1)
                    A(picks[:, :], picks[:, :], ACT.Exp).then_inc(pick_exp, 1)
                    act.wait_ge(selT_done, L * TB + b + 1)
                    A(selT[:, :, :].rearrange("p a b -> p (a b)"), ps[:, 4, 0:3 * P], ACT.Copy).then_inc(selT_ready, 1)
                    act.wait_ge(g_stored, (L * TB + b) * 16)
                    for g in range(P // 4):
                        act.wait_ge(rows_free, (L * TB + b) * P + (4 * g + 4 + HROWS))
                        A(gbuf[:, :, 4 * g:4 * g + 4], ps[:, g % 4, :].rearrange("p (t n) -> p n t", t=4), ACT.Copy).then_inc(g_copied, 1)
                act.wait_ge(g_stored, (L + 1) * (TB * 16))
                with act.Fori(0, PAIRS // 2) as j:
                    for k in range(2):
                        n = act.snap(j * 2 + k)
                        act.wait_ge(w_ready, L * NK + n * 2)
                        for s in range(2):
                            act.wait_ge(used[s], L * SLOT_USES + n + (FIRST + 1))
                            A(act_e[:, s, :], ps[:, s, :], ACT.Gelu).then_inc(gelu_ready, 1)
                        for m in range(2):
                            act.wait_ge(w_ready, L * NK + n * 2 + (m + 1))
                            A(eh[:, k, m, :], weighted[:, m, :], ACT.Copy).then_inc(eh_ready, 1)
            act.wait_ge(acc_done, LAYERS * ACC)
            norm(LAYERS, 0, lambda c: h[:, c, :], T, None)

        @block.vector
        def _(dve):
            V = nc.vector
            TT, TS, STT = V.tensor_tensor, V.tensor_scalar, V.scalar_tensor_tensor
            drain = dve.drain

            def panel(s, L, use):
                dve.wait_ge(used[s], L * (SLOT_USES if s < 2 else FIRST) + use + 1)

            def hold(s_, n):
                dve.wait_ge(s_, n)
                dve.nop(nofuse=True)

            def norm(L, k, src, w, g, lo, hi):
                dve.wait_ge(std_ready, L * 4 + k + 1)
                V.reciprocal(std[:, 0:w], std[:, 0:w])
                drain()

                def low(c):
                    dve.wait_ge(xhi_ready, L * NORMS + k * KC + c + 1)
                    TT(lo[:, c, :], xf[:, c % 2, 0:w], hi[:, c, :].bitcast(F32), ALU.subtract).then_inc(xlo_ready, 1)

                for c in range(KC):
                    if c >= 2:
                        drain()
                    STT(out=xf[:, c % 2, 0:w], in0=src(c), scalar=pc(g, c), in1=std[:, 0:w], op0=ALU.mult, op1=ALU.mult).then_inc(xf_ready, 1)
                    if c:
                        low(c - 1)
                low(KC - 1)
                drain()

            V.memset(small[:, 0:1], 1e-6).then_inc(consts_ready, 1)
            V.memset(small[:, 1:2], 1e-5).then_inc(consts_ready, 1)
            V.memset(cpad[:, 0:2], 0.0).then_inc(rows_free, HROWS)
            dve.wait_ge(const_loaded, 16)
            V.tensor_copy(identb[:, :], cst("ident")).then_inc(consts_ready, 1)
            V.tensor_copy(negmaskb[:, :], cst("negmask")).then_inc(consts_ready, 1)
            dve.wait_ge(x_loaded, 16)
            dve.nop(nofuse=True)
            with dve.Fori(0, LAYERS) as L:
                drain()
                dve.wait_ge(par_loaded, (L + 1) * 16)
                for ct in range(SB_TILES):
                    V.memset(upad[:, ct, 0:CV_TAPS - 1], 0.0)
                V.memset(cpad[:, 0:SC_TAPS - 1], 0.0)
                norm(L, 0, lambda c: h[:, c, :], T, "mix_g", xlo, xhi)

                def cv(ct):
                    dve.wait_ge(cv_sig, L * SB_TILES + ct + 1)
                    TT(upad[:, ct, 30:30 + T], ps[:, (2 * ct) % 4, :], xf[:, ct % 2, :], ALU.mult).then_inc(cv_u, 1)

                def taps(ct, lo, hi):
                    for k in range(lo, hi):
                        drain()
                        w = pc("cw", ct * CV_TAPS + k)
                        if k == 0:
                            ins = TS(conv[:, ct, :], upad[:, ct, 0:T], w, pc("cb", ct), ALU.mult, ALU.add)
                        else:
                            ins = STT(out=conv[:, ct, :], in0=upad[:, ct, k:k + T], scalar=w, in1=conv[:, ct, :], op0=ALU.mult, op1=ALU.add)
                    if hi == CV_TAPS:
                        ins.then_inc(conv_ready, 1)

                def sc(ct):
                    b0, x0 = 8 + 3 * ct, 8 + 3 * ct + 2
                    dve.wait_ge(sc_copied, L * SB_TILES + ct + 1)
                    panel(x0 % 4, L, 3 + x0 // 4)
                    TT(cpad[:, 2:2 + T], ps[:, x0 % 4, :], sc_c[:, :], ALU.mult).then_inc(sc_cx, 1)
                    drain()
                    TS(sc_o[:, :], cpad[:, 0:T], pc("scw", ct * SC_TAPS), None, ALU.mult)
                    for k in range(1, SC_TAPS):
                        drain()
                        STT(out=sc_o[:, :], in0=cpad[:, k:k + T], scalar=pc("scw", ct * SC_TAPS + k), in1=sc_o[:, :], op0=ALU.mult, op1=ALU.add)
                    drain()
                    TT(yt[:, ct % 2, :], ps[:, b0 % 4, :], sc_o[:, :], ALU.mult).then_inc(sc_y, 1)

                def sc_lo(ct):
                    dve.wait_ge(shi_ready, L * SB_TILES + ct + 1)
                    TT(blo[:, 8 + ct, :], yt[:, ct % 2, :], bhi[:, 8 + ct, :].bitcast(F32), ALU.subtract).then_inc(slo_ready, 1)

                for hd in range(SB_HEADS):
                    dve.wait_ge(ln_ready, L * SB_HEADS + hd + 1)
                    STT(out=sp[:, :], in0=zps[:, 0:ZCOLS], scalar=0.0, in1=soft[:, :], op0=ALU.max, op1=ALU.add).then_inc(sp_ready, 1)
                    if hd >= 1:
                        taps((hd - 1) // 2, *((0, 16) if (hd - 1) % 2 == 0 else (16, CV_TAPS)))
                    if hd < 4:
                        cv(hd)
                    if hd >= 6:
                        sc_lo(hd - 6)
                    if hd >= 5:
                        drain()
                        sc(hd - 5)
                    if hd % 2:
                        dve.wait_ge(yhi_ready, L * SB_TILES + hd // 2 + 1)
                        TT(blo[:, hd // 2, :], ps[:, 7, :], bhi[:, hd // 2, :].bitcast(F32), ALU.subtract).then_inc(ylo_ready, 1)
                taps(3, 16, CV_TAPS)
                sc_lo(2)
                drain()
                sc(3)
                sc_lo(3)
                dve.wait_ge(mu_done, L + 1)
                for ct in range(SB_TILES):
                    STT(out=conv[:, ct, :], in0=ps[:, 6, :], scalar=-1.0 / (SB_TILES * P), in1=conv[:, ct, :],
                        op0=ALU.mult, op1=ALU.add).then_inc(dev_ready, 1)
                dve.wait_ge(ln_std, L + 1)
                V.reciprocal(std[:, :], std[:, :])
                drain()
                for ct in range(SB_TILES):
                    TT(conv[:, ct, :], conv[:, ct, :], std[:, :], ALU.mult).then_inc(ln_scaled, 1)
                for ct in range(SB_TILES):
                    dve.wait_ge(chi_ready, L * SB_TILES + ct + 1)
                    TT(blo[:, 4 + ct, :], conv[:, ct, :], bhi[:, 4 + ct, :].bitcast(F32), ALU.subtract).then_inc(clo_ready, 1)
                drain()
                with dve.Fori(0, KC) as dt:
                    for b in range(3):
                        dve.wait_ge(gate_sig, (L * KC + dt) * 3 + (b + 1))
                        if b < 2:
                            dve.wait_ge(br_done, (L * KC + dt) * 2 + (b + 1))
                        else:
                            dve.wait_ge(used[3], L * FIRST + dt + (FRONT // 4 + 1))
                        TT(sg[:, b, :], ps[:, 3 + b, :], sg[:, b, :], ALU.mult).then_inc(br_used, 1)
                        if b:
                            drain()
                            TT(sg[:, 0, :], sg[:, 0, :], sg[:, b, :], ALU.add)
                    drain()
                    V.tensor_copy(mghi[:, dt, :], sg[:, 0, :])
                    drain()
                    TT(mglo[:, dt, :], sg[:, 0, :], mghi[:, dt, :].bitcast(F32), ALU.subtract).then_inc(mlo_ready, 1)
                drain()

                def residual(use):
                    for i in range(KC):
                        panel(i % 4, L, use + i // 4)
                        TT(h[:, i, :], h[:, i, :], ps[:, i % 4, :], ALU.add).then_inc(h_ready, 1)

                residual(FRONT // 4 + KC)
                norm(L, 1, lambda c: mem[:, c, :], N_MEM, "mem_g", mlo, mhi)
                norm(L, 2, lambda c: h[:, c, :], T, "xa_g", xlo, xhi)
                for hd in range(XA_HEADS):
                    k, a = 2 * (hd % 2), 8 + 4 * (hd % 2)
                    dve.wait_ge(xs_done, L * XA_HEADS + hd + 1)
                    V.tensor_reduce(small[:, a + 16:a + 20], ps[:, k:k + 2, :].rearrange("p a (b m) -> p (a b) m", b=2), AX.X, ALU.max)
                    drain()
                    TS(small[:, a:a + 4], small[:, a + 16:a + 20], -1.0, None, ALU.mult).then_inc(xs_neg, 1)
                    dve.wait_ge(xs_exp, (L * XA_HEADS + hd + 1) * TB)
                    V.reciprocal(small[:, a + 24:a + 28], small[:, a + 8:a + 12])
                    drain()
                    for tb in range(TB):
                        TS(prob[:, hd % 2, tb * N_MEM:(tb + 1) * N_MEM], prob[:, hd % 2, tb * N_MEM:(tb + 1) * N_MEM],
                           small[:, a + 24 + tb:a + 25 + tb], None, ALU.mult).then_inc(xs_norm, 1)
                    for c in range(2):
                        dve.wait_ge(xohi_ready, L * KC + hd * 2 + c + 1)
                        TT(olo[:, 2 * hd + c, :], ps[:, 6 + c, :], ohi[:, 2 * hd + c, :].bitcast(F32), ALU.subtract).then_inc(xolo_ready, 1)
                residual(FRONT // 4 + KC + 8)
                norm(L, 3, lambda c: h[:, c, :], T, "ffn_g", xlo, xhi)
                for l in range(LISTS):
                    hold(score_done, L * LISTS + l + 1)
                    scores = [ps[:, 4 + l % 4, tb * NK:(tb + 1) * NK] for tb in range(TB)]
                    for tb in range(TB):
                        V.max(vals[:, tb, l, 0:8], scores[tb])
                    drain()
                    for tb in range(TB):
                        V.match_replace(rest[:, tb, :], vals[:, tb, l, 0:8], scores[tb], NEG)
                    for tb in range(TB):
                        V.max_index(inds[:, tb, l, 0:8], vals[:, tb, l, 0:8], scores[tb]).then_inc(score_used, 1)
                    drain()
                    for tb in range(TB):
                        V.max(vals[:, tb, l, 8:16], rest[:, tb, :])
                    drain()
                    for tb in range(TB):
                        V.max_index(inds[:, tb, l, 8:16], vals[:, tb, l, 8:16], rest[:, tb, :])
                    drain()
                with dve.Fori(0, TB) as b:
                    v4 = vals[:, b, :, :].rearrange("p (h q) k -> p h q k", q=2)
                    i4 = inds[:, b, :, :].rearrange("p (h q) k -> p h q k", q=2)
                    dve.wait_ge(rows_free, (L * TB + b) * P + HROWS)
                    TT(cand[:, :, :].rearrange("p h (i j) -> p h i j", i=TOPK),
                       v4[:, :, 0, :].unsqueeze(3).to_broadcast([P, PH, TOPK, TOPK]),
                       v4[:, :, 1, :].unsqueeze(2).to_broadcast([P, PH, TOPK, TOPK]), ALU.add)
                    drain()
                    first = [slice(hd * TOPK, hd * TOPK + 8) for hd in range(PH)]
                    second = [slice(hd * TOPK + 8, (hd + 1) * TOPK) for hd in range(PH)]
                    for hd in range(PH):
                        V.max(picks[:, first[hd]], cand[:, hd, :])
                    drain()
                    for hd in range(PH):
                        V.max_index(pick_i[:, first[hd]], picks[:, first[hd]], cand[:, hd, :])
                    drain()
                    for hd in range(PH):
                        V.match_replace(cand[:, hd, :], picks[:, first[hd]], cand[:, hd, :], NEG)
                    drain()
                    for hd in range(PH):
                        V.max(picks[:, second[hd]], cand[:, hd, :])
                    drain()
                    for hd in range(PH):
                        V.max_index(pick_i[:, second[hd]], picks[:, second[hd]], cand[:, hd, :])
                    p3 = picks[:, :].rearrange("p (h k) -> p h k", k=TOPK)
                    V.tensor_copy(small[:, 40:48], p3[:, :, 0])
                    drain()
                    TT(p3, p3, small[:, 40:48].unsqueeze(2).to_broadcast([P, PH, TOPK]), ALU.subtract).then_inc(pick_diff, 1)
                    TS(rank[:, 0, :], pick_i[:, :], 4, None, ALU.logical_shift_right)
                    TS(rank[:, 1, :], pick_i[:, :], TOPK - 1, None, ALU.bitwise_and)
                    l4 = lookup[:, :, :].rearrange("p (h k) j -> p h k j", h=PH)
                    for q in range(2):
                        drain()
                        TT(lookup[:, :, :], rank[:, q, :].unsqueeze(2).to_broadcast([P, SEL, TOPK]),
                           cst("iota16", TOPK).unsqueeze(1).to_broadcast([P, SEL, TOPK]), ALU.is_equal)
                        drain()
                        TT(l4, l4, i4[:, :, q, :].unsqueeze(2).to_broadcast([P, PH, TOPK, TOPK]), ALU.mult)
                        drain()
                        V.tensor_reduce(eidx[:, q, :], lookup[:, :, :], AX.X, ALU.add)
                    dve.wait_ge(pick_exp, L * TB + b + 1)
                    V.tensor_reduce(small[:, 48:56], p3, AX.X, ALU.add)
                    drain()
                    V.reciprocal(small[:, 40:48], small[:, 48:56])
                    drain()
                    TT(eidx[:, 2, :].rearrange("p (h k) -> p h k", k=TOPK), p3,
                       small[:, 40:48].unsqueeze(2).to_broadcast([P, PH, TOPK]), ALU.mult).then_inc(pick_ready, 1)
                    dve.wait_ge(selT_ready, L * TB + b + 1)
                    dve.nop(nofuse=True)
                    with dve.Fori(0, P // HROWS) as g:
                        for k in range(HROWS):
                            t = dve.snap(g * HROWS + k)
                            dve.wait_ge(rows_free, (L * TB + b) * P + g * HROWS + (k + 1))
                            TS(onehot2[:, k, :], cst("iota"), selT[:, 1, bass.ds(t, 1)], None, ALU.is_equal)
                            TS(onehot1[:, k, :], cst("iota"), selT[:, 0, bass.ds(t, 1)], selT[:, 2, bass.ds(t, 1)],
                               ALU.is_equal, ALU.mult).then_inc(rows_ready, 1)

                def weigh(k, n, loads):
                    drain()
                    dve.wait_ge(gt_loaded[k], loads * 16)
                    dve.wait_ge(eh_ready, L * NK + n * 2)
                    for m in range(2):
                        dve.wait_ge(gelu_ready, L * NK + n * 2 + (m + 1))
                        TT(weighted[:, m, :], act_e[:, m, :], gtile[:, k, m, :], ALU.mult).then_inc(w_ready, 1)
                    for m in range(2):
                        dve.wait_ge(eh_ready, L * NK + n * 2 + (m + 1))
                        TT(el[:, k, m, :], weighted[:, m, :], eh[:, k, m, :].bitcast(F32), ALU.subtract).then_inc(el_ready, 1)

                def gather(n):
                    for c in range(KC):
                        dve.wait_ge(v_done, (L * PAIRS + n) * KC + (c + 1))
                        TT(h[:, c, :], h[:, c, :], ps[:, 2 + c % 6, :], ALU.add).then_inc(acc_done, 1)

                hold(g_stored, (L + 1) * (TB * 16))
                HALF = PAIRS // 2
                weigh(0, L * 0, L * HALF + 1)
                with dve.Fori(0, HALF - 1) as j:
                    weigh(1, j * 2 + 1, L * HALF + j + 1)
                    gather(j * 2)
                    weigh(0, j * 2 + 2, L * HALF + j + 2)
                    gather(j * 2 + 1)
                weigh(1, L * 0 + (PAIRS - 1), (L + 1) * HALF)
                gather(L * 0 + (PAIRS - 2))
                gather(L * 0 + (PAIRS - 1))
            dve.wait_ge(std_ready, LAYERS * 4 + 1)
            V.reciprocal(std[:, :], std[:, :])
            drain()
            for c in range(KC):
                STT(out=h[:, c, :], in0=h[:, c, :], scalar=pc("fin_g", c), in1=std[:, :], op0=ALU.mult, op1=ALU.mult).then_inc(out_ready, 1)

        @block.tensor
        def _(pe):
            MM, TR = nc.tensor.matmul, nc.tensor.transpose

            def linear(s, L, use, out, ahi, alo, chunks=range(KC), w0=0, done=None):
                pe.wait_ge(split[s], L * SLOT_USES + use + 1)
                for i, c in enumerate(chunks):
                    a = SLOT[s] + (w0 + i) * P
                    for n, (w, x) in enumerate(((whi, ahi), (whi, alo), (wlo, ahi))):
                        ins = MM(out, w[:, a:a + P], x[:, c, :], start=(i == 0 and n == 0), stop=(i == len(chunks) - 1 and n == 2))
                ins.then_inc(used[s] if done is None else done, 1)

            def norm(L, k, w):
                for c in range(KC):
                    pe.wait_ge(sq_ready, L * NORMS + k * KC + c + 1)
                    MM(ps[:, 7, 0:w], cst("ones"), sq[:, c % 2, 0:w], start=(c == 0), stop=(c == KC - 1)).then_inc(sq_used, 1)

            pe.wait_ge(consts_ready, 4)
            pe.nop(nofuse=True)
            with pe.Fori(0, LAYERS) as L:
                pe.wait_ge(acc_done, L * ACC)
                norm(L, 0, T)
                pe.wait_ge(xlo_ready, L * NORMS + KC)
                pe.nop(nofuse=True)
                with pe.Fori(0, 3) as i:
                    for s in range(4):
                        pe.wait_ge(qkv_copied, L * 12 + i * 4)
                        linear(s, L, i, ps[:, s, :], xhi, xlo)
                pe.wait_ge(qkv_copied, (L + 1) * 12)
                for b in range(TB):
                    for t in range(SB_TILES):
                        ins = TR(ps[:, 4 + b, t * P:(t + 1) * P], vT[:, t, b * P:(b + 1) * P], cst("ident"))
                    ins.then_inc(vt_done, 1)
                pe.wait_ge(vt_copied, (L + 1) * TB)

                def front(n):
                    if 4 <= n < 8:
                        pe.wait_ge(cv_u, L * SB_TILES + n // 2 - 1)
                    elif 8 <= n < 12:
                        pe.wait_ge(cv_u, L * SB_TILES + (4 if n >= 10 else 3))
                    elif n >= 12:
                        tile, which = divmod(n - 12, 3)
                        pe.wait_ge((sc_y, sc_copied, sc_cx)[which], L * SB_TILES + tile + 1)
                    linear(n % 4, L, 3 + n // 4, ps[:, n % 4, :], xhi, xlo)

                for hd in range(SB_HEADS):
                    r, tile = 64 * (hd % 2), hd // 2
                    pe.wait_ge(a_ready, L * SB_HEADS + hd)
                    for sb in range(TB):
                        z = zps[:, ZO[sb]:ZO[sb] + ZW[sb]]
                        MM(z, kT[r:r + 64, tile, sb * P:(sb + 1) * P], qT[r:r + 64, tile, sb * P:T], start=(sb != 3), stop=False, skip_group_check=True)
                        ins = MM(z[:, 0:P], identb[:, :], negmaskb[:, :], start=False, stop=False, skip_group_check=True)
                    ins.then_inc(z_done, 1)
                    front(2 * hd)
                    pe.wait_ge(sp_ready, L * SB_HEADS + hd + 1)
                    for sb in range(TB - 1, -1, -1):
                        z = zps[:, ZO[sb]:ZO[sb] + ZW[sb]]
                        for sj in range(sb + 1, TB):
                            MM(z[:, ZW[sb] - ZW[sj]:], cst("negones"), sp[:, ZO[sj]:ZO[sj] + ZW[sj]], start=False, stop=False, skip_group_check=True)
                        ins = MM(z, cst("tri"), sp[:, ZO[sb]:ZO[sb] + ZW[sb]], start=False, stop=True, skip_group_check=True)
                    ins.then_inc(c_done, 1)
                    front(2 * hd + 1)
                    pe.wait_ge(a_ready, L * SB_HEADS + hd + 1)
                    pe.wait_ge(ylo_ready, L * SB_TILES + tile)
                    for sb in range(TB):
                        ins = MM(ps[r:r + 64, 7, sb * P:T], vtok[:, sb, hd * 64:(hd + 1) * 64], soft[:, ZO[sb]:ZO[sb] + ZW[sb]],
                                 start=(sb == 0), stop=(sb == TB - 1), skip_group_check=True)
                    ins.then_inc(y_done, 1)
                for n in range(16, 20):
                    front(n)
                pe.wait_ge(conv_ready, (L + 1) * SB_TILES)
                for ct in range(SB_TILES):
                    ins = MM(ps[:, 6, :], cst("ones"), conv[:, ct, :], start=(ct == 0), stop=(ct == SB_TILES - 1))
                ins.then_inc(mu_done, 1)
                pe.wait_ge(ylo_ready, (L + 1) * SB_TILES)
                for ct in range(SB_TILES):
                    pe.wait_ge(dsq_ready, L * SB_TILES + ct + 1)
                    MM(ps[:, 7, :], cst("ones"), sq[:, ct % 2, :], start=(ct == 0), stop=(ct == SB_TILES - 1)).then_inc(var_done, 1)
                pe.wait_ge(slo_ready, (L + 1) * SB_TILES)
                pe.nop(nofuse=True)
                with pe.Fori(0, KC) as dt:
                    pe.wait_ge(gate_sig, (L * KC + dt) * 3)
                    for b in range(3):
                        linear(b, L, dt + FRONT // 4, ps[:, b, :], xhi, xlo)
                    pe.wait_ge(clo_ready, (L + 1) * SB_TILES)
                    pe.wait_ge(br_used, (L * KC + dt) * 3)
                    for b in range(3):
                        linear(3, L, dt + FRONT // 4, ps[:, 3 + b, :], bhi, blo, range(4 * b, 4 * b + 4), 4 * b, None if b == 2 else br_done)
                pe.wait_ge(mlo_ready, (L + 1) * KC)
                for i in range(2):
                    for s in range(4):
                        pe.wait_ge(h_ready, L * ROUNDS + i * 4)
                        linear(s, L, FRONT // 4 + KC + i, ps[:, s, :], mghi, mglo)
                    if i == 0:
                        norm(L, 1, N_MEM)
                pe.wait_ge(std_ready, L * 4 + 2)
                norm(L, 2, T)
                pe.wait_ge(h_ready, L * ROUNDS + KC)
                pe.wait_ge(xlo_ready, L * NORMS + 2 * KC)
                pe.nop(nofuse=True)
                with pe.Fori(0, 4) as i:
                    for s in range(4):
                        pe.wait_ge(kv_copied, L * 16 + i * 4)
                        linear(s, L, i + (FRONT // 4 + KC + 2), ps[:, s, 0:N_MEM], mhi, mlo)
                pe.wait_ge(kv_copied, (L + 1) * 16)
                pe.wait_ge(std_ready, L * 4 + 3)
                for m in range(MB):
                    for c in range(KC):
                        ins = TR(ps[:, 4 + 2 * m + c // 4, (c % 4) * P:(c % 4 + 1) * P], xvT[:, c, m * P:(m + 1) * P], cst("ident"))
                    ins.then_inc(xvt_done, 1)
                pe.wait_ge(xlo_ready, L * NORMS + 3 * KC)
                pe.nop(nofuse=True)
                with pe.Fori(0, 2) as i:
                    for s in range(4):
                        pe.wait_ge(xq_copied, L * 8 + i * 4)
                        linear(s, L, i + (FRONT // 4 + KC + 6), ps[:, s, :], xhi, xlo)
                pe.wait_ge(xq_copied, (L + 1) * 8)
                pe.wait_ge(xvt_copied, (L + 1) * MB)

                def xa_scores(hd):
                    k = 2 * (hd % 2)
                    for tb in range(TB):
                        for c in range(2):
                            ins = MM(ps[:, k + tb // 2, (tb % 2) * N_MEM:(tb % 2 + 1) * N_MEM],
                                     xqT[:, 2 * hd + c, tb * P:(tb + 1) * P], xkT[:, 2 * hd + c, :], start=(c == 0), stop=(c == 1))
                    ins.then_inc(xs_done, 1)

                xa_scores(0)
                for hd in range(XA_HEADS):
                    if hd + 1 < XA_HEADS:
                        pe.wait_ge(xs_exp, (L * XA_HEADS + hd) * TB)
                        xa_scores(hd + 1)
                    pe.wait_ge(xs_norm, (L * XA_HEADS + hd + 1) * TB)
                    pe.wait_ge(xt_copied, L * (XA_HEADS * MB) + hd * MB)
                    for m in range(MB):
                        for tb in range(TB):
                            a = tb * N_MEM + m * P
                            ins = TR(ps[:, 4 + m, tb * P:(tb + 1) * P], prob[:, hd % 2, a:a + P], cst("ident"))
                        ins.then_inc(xt_done, 1)
                    pe.wait_ge(xt_copied, L * (XA_HEADS * MB) + (hd + 1) * MB)
                    pe.wait_ge(xolo_ready, L * KC + 2 * hd)
                    for c in range(2):
                        for m in range(MB):
                            ins = MM(ps[:, 6 + c, :], xv[:, m, (2 * hd + c) * P:(2 * hd + c + 1) * P], probT[:, m, :], start=(m == 0), stop=(m == MB - 1))
                        ins.then_inc(xo_done, 1)
                pe.wait_ge(xolo_ready, (L + 1) * KC)
                pe.wait_ge(xs_exp, (L + 1) * (XA_HEADS * TB))
                pe.nop(nofuse=True)
                with pe.Fori(0, 2) as i:
                    for s in range(4):
                        pe.wait_ge(h_ready, L * ROUNDS + i * 4 + KC)
                        linear(s, L, i + (FRONT // 4 + KC + 8), ps[:, s, :], ohi, olo)
                norm(L, 3, T)
                pe.wait_ge(h_ready, (L + 1) * ROUNDS)
                pe.wait_ge(std_ready, L * 4 + 4)
                pe.wait_ge(xlo_ready, L * NORMS + 4 * KC)
                pe.wait_ge(keys_loaded, (L + 1) * 16)

                def query(l):
                    if l >= 4:
                        pe.wait_ge(pq_copied, L * LISTS + l - 3)
                    linear(l % 4, L, FRONT // 4 + KC + 10 + l // 4, ps[:, l % 4, :], xhi, xlo)

                def score(l):
                    pe.wait_ge(pq_copied, L * LISTS + l + 1)
                    if l >= 4:
                        pe.wait_ge(score_used, (L * LISTS + l - 3) * TB)
                    for tb in range(TB):
                        ins = MM(ps[:, 4 + l % 4, tb * NK:(tb + 1) * NK], pqT[:, l % 2, tb * P:(tb + 1) * P], keys[:, l, :], start=True, stop=True)
                    ins.then_inc(score_done, 1)

                query(0)
                for l in range(1, LISTS):
                    query(l)
                    score(l - 1)
                score(LISTS - 1)
                with pe.Fori(0, TB) as b:
                    pe.wait_ge(score_used, (L + 1) * (LISTS * TB))
                    pe.wait_ge(pick_ready, L * TB + b + 1)
                    for q in range(3):
                        ins = TR(ps[:, 4, q * P:(q + 1) * P], eidx[:, q, :], cst("ident"))
                    ins.then_inc(selT_done, 1)
                    with pe.Fori(0, P // 16) as g:
                        for k in range(16):
                            if k % 4 == 0:
                                pe.wait_ge(g_copied, (L * TB + b) * (P // 4) + g * 4)
                            pe.wait_ge(rows_ready, (L * TB + b) * P + g * 16 + (k + 1))
                            MM(ps[:, k // 4, (k % 4) * NK:(k % 4 + 1) * NK], onehot2[:, k % HROWS, :], onehot1[:, k % HROWS, :],
                               start=True, stop=True).then_inc(rows_free, 1)
                pe.wait_ge(g_copied, (L + 1) * (TB * P // 4))

                def up(n):
                    pe.wait_ge(gelu_ready, L * NK + n * 2)
                    for s in range(2):
                        linear(s, L, n + FIRST, ps[:, s, :], xhi, xlo)

                def down(k, n):
                    pe.wait_ge(el_ready, L * NK + n * 2 + 2)
                    for s in (2, 3):
                        pe.wait_ge(split[s], L * SLOT_USES + n + (FIRST + 1))
                    for c in range(KC):
                        if c == 0:
                            pe.wait_ge(acc_done, (L * PAIRS + n) * KC)
                        if c >= 6:
                            pe.wait_ge(acc_done, (L * PAIRS + n) * KC + (c - 5))
                        for m in range(2):
                            a = SLOT[2 + m] + c * P
                            for q, (w, x) in enumerate(((whi, eh), (whi, el), (wlo, eh))):
                                ins = MM(ps[:, 2 + c % 6, :], w[:, a:a + P], x[:, k, m, :], start=(m == 0 and q == 0), stop=(m == 1 and q == 2))
                        ins.then_inc(v_done, 1)

                up(L * 0)
                with pe.Fori(0, PAIRS // 2 - 1) as j:
                    up(j * 2 + 1)
                    down(0, j * 2)
                    up(j * 2 + 2)
                    down(1, j * 2 + 1)
                up(L * 0 + (PAIRS - 1))
                down(0, L * 0 + (PAIRS - 2))
                down(1, L * 0 + (PAIRS - 1))
            norm(LAYERS, 0, T)


def kernel(**inputs):
    import numpy as np
    import concourse.bacc as bacc
    from concourse.bass_utils import run_bass_kernel_spmd

    a = {k: np.ascontiguousarray(v) for k, v in inputs.items()}

    def rows(w):
        lead, (K, N) = w.shape[:-2], w.shape[-2:]
        w = w.reshape(*lead, K // P, P, N // P, P)
        n = len(lead)
        return np.ascontiguousarray(w.transpose(*range(n), n + 2, n + 1, n, n + 3)).reshape(*lead, N // P, P, K)

    def cols(v):
        return v.reshape(LAYERS, -1, P).transpose(0, 2, 1)

    w_in = rows(a["w_in"])
    cv, sc, gate = w_in[:, 12:20], w_in[:, 20:32], w_in[:, 32:56]
    cv = cv[:, [0, 4, 1, 5, 2, 6, 3, 7]]
    sc = sc[:, [0, 4, 8, 1, 5, 9, 2, 6, 10, 3, 7, 11]]
    gate = gate[:, [b * KC + dt for dt in range(KC) for b in range(3)]]
    branch = rows(a["w_branch"]).transpose(0, 2, 3, 1, 4)
    par = np.concatenate([
        cols(a["norm_mix_g"]), cols(a["norm_xa_g"]), cols(a["norm_mem_g"]), cols(a["norm_ffn_g"]),
        a["conv_dw_w"].reshape(LAYERS, CV_TAPS, SB_TILES, P).transpose(0, 3, 2, 1).reshape(LAYERS, P, -1),
        cols(a["conv_dw_b"]), cols(a["conv_ln_g"]), cols(a["conv_ln_b"]),
        a["sc_w"].reshape(LAYERS, SC_TAPS, SB_TILES, P).transpose(0, 3, 2, 1).reshape(LAYERS, P, -1),
        cols(a["b_gate"]), np.stack([a["final_g"].reshape(KC, P).T] * LAYERS)], axis=2)
    i = np.arange(P, dtype=np.float32)
    low = (i[:, None] >= i[None, :]).astype(np.float32)
    const = np.concatenate([
        np.eye(P, dtype=np.float32), np.ones((P, P), np.float32), -np.ones((P, P), np.float32),
        -low, np.tile(i, (P, 1)), low * np.float32(-1e30), np.tile(i[:TOPK], (P, 1))], axis=1)
    L = LAYERS
    data = {
        "xT": a["x"][0].T.reshape(KC, P, T).transpose(1, 0, 2),
        "memT": a["mem"][0].T.reshape(KC, P, N_MEM).transpose(1, 0, 2),
        "par": par,
        "const": const,
        "front": np.concatenate([w_in[:, 0:12], cv, sc], axis=1).reshape(L * FRONT, P, D),
        "gates": gate.reshape(L * GATES, P, D),
        "branch": branch.reshape(L * KC, P, 12 * P),
        "back": np.concatenate([rows(a[n]) for n in ("w_out", "xa_wkv", "xa_wq", "xa_wo", "peer_wq")], axis=1).reshape(L * BACK, P, D),
        "keys": a["peer_keys"].reshape(L, LISTS, NK, P).transpose(0, 3, 1, 2),
        "u": rows(a["peer_u"].transpose(0, 2, 1)).reshape(L * NK, P, D),
        "v": a["peer_v"].reshape(L * NK, P, D),
    }
    nc = bacc.Bacc("TRN2", target_bir_lowering=False, num_devices=1)
    arrays, args = {}, []
    for name, v in data.items():
        v = np.ascontiguousarray(v)
        arrays[f"in_{name}"] = v
        args.append(nc.dram_tensor(f"in_{name}", v.shape, mybir.dt.from_np(v.dtype), kind="ExternalInput").ap())
    out = nc.dram_tensor("out", (P, KC, T), F32, kind="ExternalOutput").ap()
    build_trunk(nc, *args, out)
    r = run_bass_kernel_spmd(nc, [arrays], core_ids=[0])
    return r.results[0]["out"].transpose(2, 1, 0).reshape(1, T, D)
```

```python
from contextlib import ExitStack

import concourse.bass as bass
from concourse import mybir

P = 128
T = 512
D = 1024
KC = D // P
LAYERS = 2
TB = T // P
N_MEM = 256
MB = N_MEM // P
SB_TILES = 4
SB_HEADS = 8
CV_TAPS = 31
SC_TAPS = 3
XA_HEADS = 4
XA_DH = D // XA_HEADS
PH = 8
LISTS = 2 * PH
NK = 128
TOPK = 16
SEL = PH * TOPK
NEG = -3.0e38

PAR, PAR_COLS = {}, 0
for _n, _c in (("mix_g", KC), ("xa_g", KC), ("mem_g", KC), ("ffn_g", KC), ("cw", SB_TILES * CV_TAPS),
               ("cb", SB_TILES), ("lng", SB_TILES), ("lnb", SB_TILES), ("scw", SB_TILES * SC_TAPS),
               ("bg", 3 * KC), ("fin_g", KC)):
    PAR[_n] = PAR_COLS
    PAR_COLS += _c

FRONT = 12 + 8 + 12
BACK = 8 + 16 + 8 + 8 + 16
GATES = 3 * KC
PAIRS = NK // 2
FIRST = FRONT // 4 + KC + BACK // 4
LEAD, WITH, BEHIND = 4, P // 16, 3
EARLY = LEAD + TB * (WITH + BEHIND)
ROUND = "vvuvvvvuvv"
RV, RU = ROUND.count("v"), ROUND.count("u")
NROUNDS = PAIRS // RV
assert EARLY == NROUNDS * (RV - RU) and len(ROUND) % 2 == 0
LATE = NROUNDS * len(ROUND) // 2
SPLITS = [FIRST + EARLY + LATE] * 2 + [FIRST + LATE] * 2
USED = [FIRST + EARLY + NROUNDS] * 2 + [FIRST + NROUNDS] * 2
G1 = FRONT // 4 + KC
ROUNDED = [KC - 1 + 9 + n - FIRST for n in SPLITS[:3]] + [9 + SPLITS[3] - FIRST]
STREAM = 2 * (EARLY + PAIRS + NROUNDS * RU)
PIECES = 4
HROWS = 8
ROUNDS = 2 * KC

F32 = mybir.dt.float32
F32R = mybir.dt.float32r
BF16 = mybir.dt.bfloat16
U32 = mybir.dt.uint32
ACT = mybir.ActivationFunctionType
ALU = mybir.AluOpType
AX = mybir.AxisListType

ZW = [T - P * sb for sb in range(TB)]
ZO = [0, 512, 1024, 896]
ZCOLS = sum(ZW)
CONSTS = ("ident", "ones", "negones", "tri", "iota", "negmask", "iota16")


def build_trunk(nc, xT, memT, par_d, const_d, front_d, gates_d, branch_d, back_d, keys_d, expert_d, outT):
    gate_d = nc.dram_tensor("gate_table", (NK, P, T), F32, kind="Internal").ap()
    early_d = nc.dram_tensor("early_gelu", (2 * EARLY, P, T), F32, kind="Internal").ap()
    ctx = ExitStack()
    with ctx:
        def sem(name):
            return ctx.enter_context(nc.semaphore(name))

        top = [(nc.sbuf_base + 63) // 64 * 64]

        def region(size):
            at = top[0]
            top[0] += (size + 31) // 32 * 32
            return at

        def place(name, at, shape, dt):
            return nc.alloc_sbuf_tensor_at(name, [P] + list(shape), dt, offset=at)

        SLOT = [0, 1024, 2048, 3072]
        RING = 3 * 1024 + 1536
        RAW = region(RING * 4)
        raw = place("raw", RAW, [RING], F32)
        early = place("early", RAW + SLOT[2] * 4, [2, T], F32)
        whi = place("whi", region(RING * 4), [RING], F32R)
        wlo = place("wlo", region(RING * 4), [RING], F32R)
        h = place("h", region(KC * T * 4), [KC, T], F32)
        xhi = place("xhi", region(KC * T * 4), [KC, T], F32R)
        xlo = place("xlo", region(KC * T * 4), [KC, T], F32R)
        E = region(24 * T * 4)
        bhi = place("bhi", E, [12, T], F32R)
        blo = place("blo", E + 12 * T * 4, [12, T], F32R)
        sp = place("sp", E + 4 * T * 4, [ZCOLS], F32)
        soft = place("soft", E + 16 * T * 4, [ZCOLS], F32)
        mhi = place("mhi", E + 8192, [KC, N_MEM], F32R)
        mlo = place("mlo", E + 16384, [KC, N_MEM], F32R)
        xvT = place("xvT", E + 24576, [KC, N_MEM], F32)
        xkT = place("xkT", E + 32768, [KC, N_MEM], F32)
        xv = place("xv", E + 40960, [MB, D], F32)
        ohi = place("ohi", E, [KC, T], F32R)
        olo = place("olo", E + 16384, [KC, T], F32R)
        F = region(16 * T * 4)
        qT = place("qT", F, [SB_TILES, T], F32)
        kT = place("kT", F + 8192, [SB_TILES, T], F32)
        vT = place("vT", F + 16384, [SB_TILES, T], F32)
        conv = place("conv", F + 16384, [SB_TILES, T], F32)
        vtok = place("vtok", F + 24576, [TB, T], F32)
        sc_c = place("sc_c", F, [T], F32)
        sc_o = place("sc_o", F + 2048, [T], F32)
        yt = place("yt", F + 8192, [2, T], F32)
        mghi = place("mghi", F, [KC, T], F32R)
        mglo = place("mglo", F + 16384, [KC, T], F32R)
        xqT = place("xqT", F, [KC, T], F32)
        prob = place("prob", F + 16384, [2, TB * N_MEM], F32)
        probT = place("probT", F + 24576, [MB, T], F32)
        gbuf = place("gbuf", E, [NK, P], F32)
        keys = place("keys", E + 65536, [LISTS, NK], F32)
        onehot2 = place("onehot2", E + 65536, [HROWS, NK], F32)
        S = E + 65536 + 4096
        picks = place("picks", S, [SEL], F32)
        pick_i = place("pick_i", S + 512, [SEL], U32)
        rank = place("rank", S + 1024, [2, SEL], U32)
        eidx = place("eidx", S + 2048, [3, SEL], F32)
        vals = place("vals", E + 65536 + 8192, [TB, LISTS, TOPK], F32)
        inds = place("inds", E + 65536 + 12288, [TB, LISTS, TOPK], U32)
        act_e = place("act_e", E, [2, 2, T], F32)
        gtile = place("gtile", E + 8192, [2, 2, T], F32)
        eh = place("eh", E + 16384, [2, 2, T], F32R)
        el = place("el", E + 24576, [2, 2, T], F32R)
        weighted = place("weighted", E + 32768, [2, T], F32)
        const = place("const", region(6 * 512 + 64), [6 * P + TOPK], F32)
        identb = place("identb", region(256), [P], BF16)
        negmaskb = place("negmaskb", region(256), [P], BF16)
        par = place("par", region(PAR_COLS * 4), [PAR_COLS], F32)
        std = place("std", region(T * 4), [T], F32)
        SQ = region(4 * T * 4)
        sq = place("sq", SQ, [2, T], F32)
        xf = place("xf", SQ + 2 * T * 4, [2, T], F32)
        sg = place("sg", SQ, [3, T], F32)
        pqT = place("pqT", SQ, [2, T], F32)
        rest = place("rest", SQ + 2 * T * 4, [TB, NK], F32)
        cand = place("cand", SQ, [PH, TOPK * TOPK], F32)
        UP = region(SB_TILES * (T + 30) * 4 + (T + 2) * 4)
        upad = place("upad", UP, [SB_TILES, T + 30], F32)
        cpad = place("cpad", UP + SB_TILES * (T + 30) * 4, [T + 2], F32)
        mem = place("mem", UP, [KC, N_MEM], F32)
        lookup = place("lookup", UP, [SEL, TOPK], F32)
        selT = place("selT", SQ + HROWS * NK * 4, [3, P], F32)
        small = place("small", region(64 * 4), [64], F32)
        assert top[0] <= nc.sbuf_usable_end, (top[0], nc.sbuf_usable_end)
        onehot1 = place("onehot1", SQ, [HROWS, NK], F32)

        ps = ctx.enter_context(nc.psum_tensor("ps", [P, 8, T], F32))

        def kv_cols(i):
            return slice(i // 4 % 2 * N_MEM, (i // 4 % 2 + 1) * N_MEM)

        def cst(name, w=P):
            k = CONSTS.index(name) * P
            return const[:, k:k + w]

        def pc(name, k):
            k += PAR[name]
            return par[:, k:k + 1]

        loaded = [sem(f"loaded{s}") for s in range(4)]
        rounded = [sem(f"rounded{s}") for s in range(4)]
        split = [sem(f"split{s}") for s in range(4)]
        used = [sem(f"used{s}") for s in range(4)]
        x_loaded, par_loaded, const_loaded, mem_loaded, keys_loaded = (
            sem(n) for n in ("x_loaded", "par_loaded", "const_loaded", "mem_loaded", "keys_loaded"))
        consts_ready = sem("consts_ready")
        sq_ready, sq_used, std_ready, xf_ready, xhi_ready, xlo_ready = (
            sem(n) for n in ("sq_ready", "sq_used", "std_ready", "xf_ready", "xhi_ready", "xlo_ready"))
        h_ready = sem("h_ready")
        qkv_copied, vt_done, vt_copied = sem("qkv_copied"), sem("vt_done"), sem("vt_copied")
        z_done, ln_ready, sp_ready, c_done, a_ready, y_done = (
            sem(n) for n in ("z_done", "ln_ready", "sp_ready", "c_done", "a_ready", "y_done"))
        yhi_ready, ylo_ready = sem("yhi_ready"), sem("ylo_ready")
        cv_sig, cv_u, conv_ready = sem("cv_sig"), sem("cv_u"), sem("conv_ready")
        mu_done, dev_ready, dsq_ready, var_done, ln_std, ln_scaled, chi_ready, clo_ready = (
            sem(n) for n in ("mu_done", "dev_ready", "dsq_ready", "var_done", "ln_std", "ln_scaled", "chi_ready", "clo_ready"))
        sc_copied, sc_cx, sc_y, shi_ready, slo_ready = (
            sem(n) for n in ("sc_copied", "sc_cx", "sc_y", "shi_ready", "slo_ready"))
        gate_sig, br_done, br_used, mlo_ready = (sem(n) for n in ("gate_sig", "br_done", "br_used", "mlo_ready"))
        kv_copied, xvt_done, xvt_copied, xq_copied = (sem(n) for n in ("kv_copied", "xvt_done", "xvt_copied", "xq_copied"))
        xs_done, xs_neg, xs_exp, xs_norm, xt_done, xt_copied, xo_done, xohi_ready, xolo_ready = (
            sem(n) for n in ("xs_done", "xs_neg", "xs_exp", "xs_norm", "xt_done", "xt_copied", "xo_done", "xohi_ready", "xolo_ready"))
        pq_copied, score_done, score_used, top_ready = (sem(n) for n in ("pq_copied", "score_done", "score_used", "top_ready"))
        pick_diff, pick_exp, pick_ready, selT_done, selT_ready = (
            sem(n) for n in ("pick_diff", "pick_exp", "pick_ready", "selT_done", "selT_ready"))
        rows_ready, rows_free, g_copied, g_stored = (sem(n) for n in ("rows_ready", "rows_free", "g_copied", "g_stored"))
        gelu_ready, w_ready, eh_ready, el_ready, v_done, acc_done = (
            sem(n) for n in ("gelu_ready", "w_ready", "eh_ready", "el_ready", "v_done", "acc_done"))
        early_ready = [sem(f"early_ready{s}") for s in range(2)]
        early_stored = [sem(f"early_stored{s}") for s in range(2)]
        gt_loaded = [sem(f"gt_loaded{k}") for k in range(2)]
        act_loaded = [sem(f"act_loaded{k}") for k in range(2)]
        out_ready, out_stored = sem("out_ready"), sem("out_stored")

        block = ctx.enter_context(nc.Block())
        NORMS = 4 * KC
        ACC = PAIRS * KC
        zps = ps[:, 4:7, :].rearrange("p a b -> p (a b)")

        @block.sync
        def _(sp_):
            eng = sp_
            eng.dma_start(h[:, :, :], xT).then_inc(x_loaded, 16)
            eng.dma_start(const[:, :], const_d).then_inc(const_loaded, 16)

            def feed(s, L, use, row, src, width=1024):
                at = eng.snap(row)
                n = eng.snap(L * SPLITS[s] + use)
                eng.wait_ge(split[s], n)
                eng.dma_start(raw[:, SLOT[s]:SLOT[s] + width], src[at]).then_inc(loaded[s], 16)

            with eng.Fori(0, LAYERS) as L:
                lay = eng.snap(L * 1)
                eng.wait_ge(acc_done, L * ACC)
                eng.dma_start(par[:, :], par_d[lay]).then_inc(par_loaded, 16)
                with eng.Fori(0, FRONT // 4) as i:
                    for s in range(4):
                        feed(s, L, i, L * FRONT + i * 4 + s, front_d)
                with eng.Fori(0, KC) as i:
                    for s in range(3):
                        feed(s, L, i + FRONT // 4, L * GATES + i * 3 + s, gates_d)
                    feed(3, L, i + FRONT // 4, L * KC + i, branch_d, 1536)
                eng.wait_ge(conv_ready, (L + 1) * SB_TILES)
                eng.dma_start(mem[:, :, :], memT).then_inc(mem_loaded, 16)
                XB = (BACK - LISTS) // 4
                with eng.Fori(0, XB) as i:
                    for s in range(4):
                        feed(s, L, i + G1, L * BACK + i * 4 + s, back_d)
                for s in range(4):
                    feed(s, L, G1 + XB, L * BACK + (s + BACK - LISTS), back_d)
                lay = eng.snap(L * 1)
                eng.wait_ge(h_ready, (L + 1) * ROUNDS)
                eng.dma_start(keys[:, :, :], keys_d[lay]).then_inc(keys_loaded, 16)
                with eng.Fori(1, LISTS // 4) as i:
                    for s in range(4):
                        feed(s, L, i + (G1 + XB), L * BACK + i * 4 + (s + BACK - LISTS), back_d)
                for s in range(2):
                    feed(s, L, FIRST, L * STREAM + s, expert_d)

                def early_pair(i):
                    for s in range(2):
                        feed(s, L, i + (FIRST + 1), L * STREAM + i * 2 + (2 + s), expert_d)
                        at = eng.snap(i * 2 + s)
                        eng.wait_ge(early_ready[s], L * EARLY + i + 1)
                        eng.dma_start(early_d[at], early[:, s, :]).then_inc(early_stored[s], 16)

                def behind(b):
                    col = eng.snap(b * P)
                    eng.wait_ge(g_copied, (L * TB + b + 1) * (P // 4))
                    for q in range(PIECES):
                        n = NK // PIECES
                        eng.dma_start(gate_d[q * n:(q + 1) * n, :, bass.ds(col, P)].rearrange("a p t -> p a t"),
                                      gbuf[:, q * n:(q + 1) * n, :]).then_inc(g_stored, 16)
                        if q < BEHIND:
                            early_pair(b * (WITH + BEHIND) + (LEAD + WITH + q))

                with eng.Fori(0, LEAD) as i:
                    early_pair(i)
                with eng.Fori(0, TB) as b:
                    with eng.Fori(0, WITH) as g:
                        early_pair(b * (WITH + BEHIND) + g + LEAD)
                    behind(b)
                for s in range(2):
                    eng.wait_ge(early_stored[s], (L + 1) * (EARLY * 16))
                eng.nop(nofuse=True)
                with eng.Fori(0, LATE - 1) as i:
                    for s in range(2):
                        feed(2 + s, L, i + FIRST, L * STREAM + i * 4 + (2 * EARLY + 2 + s), expert_d)
                    for s in range(2):
                        feed(s, L, i + (FIRST + EARLY + 1), L * STREAM + i * 4 + (2 * EARLY + 4 + s), expert_d)
                for s in range(2):
                    feed(2 + s, L, FIRST + LATE - 1, L * STREAM + (STREAM - 2 + s), expert_d)
            eng.wait_ge(out_ready, KC)
            eng.dma_start(outT, h[:, :, :]).then_inc(out_stored, 16)
            eng.wait_ge(out_stored, 16)

        @block.gpsimd
        def _(pool):
            eng = nc.gpsimd

            def cut(s, L, use, width=1024):
                a, b = SLOT[s], SLOT[s] + width
                pool.wait_ge(loaded[s], (L * SPLITS[s] + use + 1) * 16)
                pool.wait_ge(used[s], L * USED[s] + use)
                pool.nop(nofuse=True)
                eng.tensor_copy(whi[:, a:b], raw[:, a:b])
                pool.drain()
                eng.tensor_tensor(wlo[:, a:b], raw[:, a:b], whi[:, a:b].bitcast(F32), ALU.subtract).then_inc(split[s], 1)

            def low(s, L, count):
                a, b = SLOT[s], SLOT[s] + 1024
                pool.wait_ge(rounded[s], L * ROUNDED[s] + count)
                eng.tensor_tensor(wlo[:, a:b], raw[:, a:b], whi[:, a:b].bitcast(F32), ALU.subtract).then_inc(split[s], 1)

            def lows(L, n, done):
                with pool.Fori(0, n) as i:
                    for s in range(4):
                        low(s, L, i + ((KC - 1 if s < 3 else 0) + done + 1))

            with pool.Fori(0, LAYERS) as L:
                pool.wait_ge(v_done, L * ACC)
                pool.nop(nofuse=True)
                with pool.Fori(0, FRONT // 4) as i:
                    for s in range(4):
                        cut(s, L, i)
                for s in range(3):
                    cut(s, L, FRONT // 4)
                cut(3, L, FRONT // 4, width=1536)
                with pool.Fori(1, KC) as i:
                    for s in range(3):
                        low(s, L, i)
                    cut(3, L, i + FRONT // 4, width=1536)
                with pool.Fori(G1, G1 + 3) as i:
                    for s in range(4):
                        cut(s, L, i)
                lows(L, 6, 0)
                with pool.Fori(G1 + 9, G1 + 11) as i:
                    for s in range(4):
                        cut(s, L, i)
                lows(L, 3, 6)
                with pool.Fori(0, EARLY) as i:
                    for s in range(2):
                        low(s, L, i + (KC - 1 + 9 + 1))
                with pool.Fori(0, LATE) as i:
                    for s in range(4):
                        low(s, L, i + ((KC - 1 if s < 3 else 0) + 9 + 1 + (EARLY if s < 2 else 0)))

        @block.scalar
        def _(act):
            A = nc.scalar.activation
            eps6, eps5 = small[:, 0:1], small[:, 1:2]

            def panel(s, L, use):
                act.wait_ge(used[s], L * USED[s] + use + 1)

            def round_panel(s, L, use):
                act.wait_ge(loaded[s], (L * SPLITS[s] + use + 1) * 16)
                A(whi[:, SLOT[s]:SLOT[s] + 1024], raw[:, SLOT[s]:SLOT[s] + 1024], ACT.Copy).then_inc(rounded[s], 1)

            def norm(L, k, src, w, hi):
                for c in range(KC):
                    n = k * KC + c
                    act.wait_ge(sq_used, L * NORMS + (n - 1 if n >= 2 else 0))
                    A(sq[:, c % 2, 0:w], src(c), ACT.Square).then_inc(sq_ready, 1)
                act.wait_ge(sq_used, L * NORMS + (k + 1) * KC)
                A(std[:, 0:w], ps[:, 7, 0:w], ACT.Sqrt, scale=1.0 / D, bias=eps6).then_inc(std_ready, 1)
                for c in range(KC if hi is not None else 0):
                    act.wait_ge(xf_ready, L * NORMS + k * KC + c + 1)
                    A(hi[:, c, :], xf[:, c % 2, 0:w], ACT.Copy).then_inc(xhi_ready, 1)

            act.wait_ge(consts_ready, 4)
            act.wait_ge(x_loaded, 16)
            with act.Fori(0, LAYERS) as L:
                act.wait_ge(par_loaded, (L + 1) * 16)
                act.wait_ge(acc_done, L * ACC)
                norm(L, 0, lambda c: h[:, c, :], T, xhi)
                for i in range(12):
                    panel(i % 4, L, i // 4)
                    A((qT, kT, vT)[i // 4][:, i % 4, :], ps[:, i % 4, :], ACT.Copy, scale=0.125 if i < 4 else 1.0).then_inc(qkv_copied, 1)
                for b in range(TB):
                    act.wait_ge(vt_done, L * TB + b + 1)
                    A(vtok[:, b, :], ps[:, 4 + b, :], ACT.Copy).then_inc(vt_copied, 1)

                def cv(ct):
                    n = 2 * ct + 1
                    panel(n % 4, L, 3 + n // 4)
                    act.wait_ge(cv_u, L * SB_TILES + max(0, ct - 1))
                    A(xf[:, ct % 2, :], ps[:, n % 4, :], ACT.Sigmoid).then_inc(cv_sig, 1)

                def sc_copy(ct):
                    n = 8 + 3 * ct + 1
                    panel(n % 4, L, 3 + n // 4)
                    act.wait_ge(sc_cx, L * SB_TILES + ct)
                    A(sc_c[:, :], ps[:, n % 4, :], ACT.Copy).then_inc(sc_copied, 1)

                def sc_hi(ct):
                    act.wait_ge(sc_y, L * SB_TILES + ct + 1)
                    A(bhi[:, 8 + ct, :], yt[:, ct % 2, :], ACT.Copy).then_inc(shi_ready, 1)

                for hd in range(SB_HEADS):
                    n = L * SB_HEADS + hd + 1
                    act.wait_ge(z_done, n)
                    A(soft[:, :], zps[:, 0:ZCOLS], ACT.Abs)
                    act.drain()
                    A(soft[:, :], soft[:, :], ACT.Exp, scale=-1.0)
                    act.drain()
                    A(soft[:, :], soft[:, :], ACT.Ln, bias=1.0).then_inc(ln_ready, 1)
                    act.wait_ge(c_done, n)
                    A(soft[:, :], zps[:, 0:ZCOLS], ACT.Exp).then_inc(a_ready, 1)
                    if hd < 4:
                        cv(hd)
                    if hd >= 5:
                        sc_copy(hd - 5)
                    if hd >= 6:
                        sc_hi(hd - 6)
                    if hd % 2:
                        act.wait_ge(y_done, n)
                        A(bhi[:, hd // 2, :], ps[:, 7, :], ACT.Copy).then_inc(yhi_ready, 1)
                sc_hi(2)
                sc_copy(3)
                sc_hi(3)
                for ct in range(SB_TILES):
                    act.wait_ge(dev_ready, L * SB_TILES + ct + 1)
                    if ct >= 2:
                        act.wait_ge(var_done, L * SB_TILES + ct - 1)
                    A(sq[:, ct % 2, :], conv[:, ct, :], ACT.Square).then_inc(dsq_ready, 1)
                act.wait_ge(var_done, (L + 1) * SB_TILES)
                A(std[:, :], ps[:, 7, :], ACT.Sqrt, scale=1.0 / (SB_TILES * P), bias=eps5).then_inc(ln_std, 1)
                for ct in range(SB_TILES):
                    act.wait_ge(ln_scaled, L * SB_TILES + ct + 1)
                    A(conv[:, ct, :], conv[:, ct, :], ACT.Silu, scale=pc("lng", ct), bias=pc("lnb", ct))
                    act.drain()
                    A(bhi[:, 4 + ct, :], conv[:, ct, :], ACT.Copy).then_inc(chi_ready, 1)
                for dt in range(KC):
                    act.wait_ge(mlo_ready, L * KC + dt)
                    for b in range(3):
                        panel(b, L, FRONT // 4 + dt)
                        A(sg[:, b, :], ps[:, b, :], ACT.Sigmoid, bias=pc("bg", b * KC + dt)).then_inc(gate_sig, 1)
                        if dt + 1 < KC:
                            round_panel(b, L, FRONT // 4 + dt + 1)
                act.wait_ge(mlo_ready, (L + 1) * KC)
                act.wait_ge(mem_loaded, (L + 1) * 16)
                norm(L, 1, lambda c: mem[:, c, :], N_MEM, mhi)
                act.wait_ge(h_ready, L * ROUNDS + KC)
                norm(L, 2, lambda c: h[:, c, :], T, xhi)
                base = FRONT // 4 + KC + 2
                for i in range(16):
                    panel(i % 4, L, base + i // 4)
                    A((xkT if i < 8 else xvT)[:, i % 8, :], ps[:, i % 4, kv_cols(i)], ACT.Copy).then_inc(kv_copied, 1)
                    round_panel(i % 4, L, base + i // 4 + 1)
                for m in range(MB):
                    act.wait_ge(xvt_done, L * MB + m + 1)
                    A(xv[:, m, :], ps[:, 4 + 2 * m:6 + 2 * m, :].rearrange("p a b -> p (a b)"), ACT.Copy).then_inc(xvt_copied, 1)
                for i in range(8):
                    panel(i % 4, L, base + 4 + i // 4)
                    A(xqT[:, i, :], ps[:, i % 4, :], ACT.Copy, scale=XA_DH ** -0.5).then_inc(xq_copied, 1)
                    round_panel(i % 4, L, base + 4 + i // 4 + 1)
                for hd in range(XA_HEADS):
                    act.wait_ge(xs_neg, L * XA_HEADS + hd + 1)
                    for tb in range(TB):
                        a = 8 + 4 * (hd % 2) + tb
                        A(prob[:, hd % 2, tb * N_MEM:(tb + 1) * N_MEM],
                          ps[:, 2 * (hd % 2) + tb // 2, (tb % 2) * N_MEM:(tb % 2 + 1) * N_MEM],
                          ACT.Exp, bias=small[:, a:a + 1], accum_out=small[:, a + 8:a + 9]).then_inc(xs_exp, 1)
                    act.wait_ge(xo_done, L * (XA_HEADS * 2) + hd * 2)
                    for m in range(MB):
                        act.wait_ge(xt_done, L * (XA_HEADS * MB) + hd * MB + m + 1)
                        A(probT[:, m, :], ps[:, 4 + m, :], ACT.Copy).then_inc(xt_copied, 1)
                    for c in range(2):
                        act.wait_ge(xo_done, L * (XA_HEADS * 2) + hd * 2 + c + 1)
                        A(ohi[:, 2 * hd + c, :], ps[:, 6 + c, :], ACT.Copy).then_inc(xohi_ready, 1)
                act.wait_ge(h_ready, (L + 1) * ROUNDS)
                norm(L, 3, lambda c: h[:, c, :], T, xhi)
                for l in range(LISTS):
                    panel(l % 4, L, base + 8 + l // 4)
                    if l >= 2:
                        act.wait_ge(score_done, L * LISTS + l - 1)
                    A(pqT[:, l % 2, :], ps[:, l % 4, :], ACT.Copy).then_inc(pq_copied, 1)
                    if l // 4 < 3 or l % 4 < 2:
                        round_panel(l % 4, L, base + 8 + l // 4 + 1)

                def early_pair(i):
                    for s in range(2):
                        panel(s, L, i + FIRST)
                        act.wait_ge(early_stored[s], (L * EARLY + i) * 16)
                        A(early[:, s, :], ps[:, 5 + s, :], ACT.Gelu).then_inc(early_ready[s], 1)
                        round_panel(s, L, i + (FIRST + 1))

                def pick_weights(b):
                    act.wait_ge(pick_diff, L * TB + b + 1)
                    A(picks[:, :], picks[:, :], ACT.Exp).then_inc(pick_exp, 1)

                def pick_turn(b):
                    act.wait_ge(selT_done, L * TB + b + 1)
                    A(selT[:, :, :].rearrange("p a b -> p (a b)"), ps[:, 4, 0:3 * P], ACT.Copy).then_inc(selT_ready, 1)

                def rows(b):
                    act.wait_ge(g_stored, (L * TB + b) * (16 * PIECES))
                    for g in range(WITH):
                        i = b * (WITH + BEHIND) + (LEAD + g)
                        for s in range(2):
                            panel(s, L, i + FIRST)
                            act.wait_ge(early_stored[s], (L * EARLY + i) * 16)
                            A(early[:, s, :], ps[:, 5 + s, :], ACT.Gelu).then_inc(early_ready[s], 1)
                            round_panel(s, L, i + (FIRST + 1))
                            for q in range(4 * g + 2 * s, 4 * g + 2 * s + 2):
                                act.wait_ge(rows_free, (L * TB + b) * P + (4 * q + 4 + HROWS))
                                A(gbuf[:, :, 4 * q:4 * q + 4], ps[:, q % 4, :].rearrange("p (t n) -> p n t", t=4), ACT.Copy).then_inc(g_copied, 1)

                for i in range(LEAD):
                    early_pair(L * 0 + i)
                    if i == 2:
                        pick_weights(L * 0)
                pick_turn(L * 0)
                with act.Fori(0, TB - 1) as b:
                    rows(b)
                    for i in range(BEHIND):
                        early_pair(b * (WITH + BEHIND) + (LEAD + WITH + i))
                        if i == 1:
                            pick_weights(b + 1)
                    pick_turn(b + 1)
                rows(L * 0 + (TB - 1))
                for i in range(BEHIND):
                    early_pair(L * 0 + (EARLY - BEHIND + i))

                def sides(j, r):
                    k, r4 = r % 2, r % 4
                    late = r4 == 3
                    first = act.snap(j * 4 + (2 * EARLY + r // 4 * 2) if late else j * 12 + (r // 4 * 6 + r4 * 2))
                    act.dma_start(gtile[:, k, :, :], gate_d[bass.ds(first, 2)].rearrange("a p t -> p a t")).then_inc(gt_loaded[k], 16)
                    if not late:
                        act.dma_start(act_e[:, k, :, :], early_d[bass.ds(first, 2)].rearrange("a p t -> p a t")).then_inc(act_loaded[k], 16)

                def round_use(j, step):
                    if step >= len(ROUND):
                        j, wrap = j + 1, len(ROUND)
                    else:
                        wrap = 0
                    before = step - 2
                    pair = 2 * (step % 2)
                    if before < 0:
                        act.wait_ge(v_done, (L * PAIRS + j * RV) * KC)
                    elif ROUND[before] == "v":
                        r = ROUND[:before].count("v")
                        act.wait_ge(v_done, (L * PAIRS + (j * RV - (RV if wrap else 0)) + (r + 1)) * KC)
                    for m in range(2):
                        if before >= 0 and ROUND[before] == "u":
                            act.wait_ge(used[pair + m], L * USED[pair + m] + j + (FIRST + 1 + (0 if pair else EARLY)))
                        round_panel(pair + m, L, j * (len(ROUND) // 2) + (FIRST + (0 if pair else EARLY) + (step - wrap) // 2))

                def late_gelu(j, r):
                    act.wait_ge(w_ready, (L * PAIRS + j * RV + (r - 1)) * 2)
                    for m in range(2):
                        s = m if r == 3 else 2 + m
                        act.wait_ge(used[s], L * USED[s] + j + (FIRST + 1 + (EARLY if r == 3 else 0)))
                        A(act_e[:, 1, m, :], ps[:, m, :], ACT.Gelu).then_inc(gelu_ready, 1)

                def high(j, r, more):
                    for m in range(2):
                        act.wait_ge(w_ready, (L * PAIRS + j * RV + r) * 2 + (m + 1))
                        A(eh[:, r % 2, m, :], weighted[:, m, :], ACT.Copy).then_inc(eh_ready, 1)
                    if more:
                        sides(*((j, r + 2) if r + 2 < RV else (j + 1, r + 2 - RV)))

                def expert_round(j, last):
                    r = 0
                    for step, what in enumerate(ROUND):
                        if step and ROUND[step - 1] == "u":
                            late_gelu(j, r + 1)
                        if not (last and step + 1 == len(ROUND)):
                            round_use(j, step + 1)
                        if what == "v":
                            r += 1
                            if r < RV:
                                high(j, r, not last or r + 2 < RV)
                            elif not last:
                                high(j + 1, 0, True)

                act.wait_ge(g_stored, (L + 1) * (TB * 16 * PIECES))
                for s in range(2):
                    act.wait_ge(early_stored[s], (L + 1) * (EARLY * 16))
                act.nop(nofuse=True)
                sides(L * 0, 0)
                sides(L * 0, 1)
                high(L * 0, 0, True)
                with act.Fori(0, NROUNDS - 1) as j:
                    expert_round(j, False)
                expert_round(L * 0 + (NROUNDS - 1), True)
            act.wait_ge(acc_done, LAYERS * ACC)
            norm(LAYERS, 0, lambda c: h[:, c, :], T, None)

        @block.vector
        def _(dve):
            V = nc.vector
            TT, TS, STT = V.tensor_tensor, V.tensor_scalar, V.scalar_tensor_tensor
            drain = dve.drain

            def panel(s, L, use):
                dve.wait_ge(used[s], L * USED[s] + use + 1)

            def hold(s_, n):
                dve.wait_ge(s_, n)
                dve.nop(nofuse=True)

            def norm(L, k, src, w, g, lo, hi):
                dve.wait_ge(std_ready, L * 4 + k + 1)
                V.reciprocal(std[:, 0:w], std[:, 0:w])
                drain()

                def low(c):
                    dve.wait_ge(xhi_ready, L * NORMS + k * KC + c + 1)
                    TT(lo[:, c, :], xf[:, c % 2, 0:w], hi[:, c, :].bitcast(F32), ALU.subtract).then_inc(xlo_ready, 1)

                for c in range(KC):
                    if c >= 2:
                        drain()
                    STT(out=xf[:, c % 2, 0:w], in0=src(c), scalar=pc(g, c), in1=std[:, 0:w], op0=ALU.mult, op1=ALU.mult).then_inc(xf_ready, 1)
                    if c:
                        low(c - 1)
                low(KC - 1)
                drain()

            V.memset(small[:, 0:1], 1e-6).then_inc(consts_ready, 1)
            V.memset(small[:, 1:2], 1e-5).then_inc(consts_ready, 1)
            V.memset(cpad[:, 0:2], 0.0).then_inc(rows_free, HROWS)
            dve.wait_ge(const_loaded, 16)
            V.tensor_copy(identb[:, :], cst("ident")).then_inc(consts_ready, 1)
            V.tensor_copy(negmaskb[:, :], cst("negmask")).then_inc(consts_ready, 1)
            dve.wait_ge(x_loaded, 16)
            dve.nop(nofuse=True)
            with dve.Fori(0, LAYERS) as L:
                drain()
                dve.wait_ge(par_loaded, (L + 1) * 16)
                for ct in range(SB_TILES):
                    V.memset(upad[:, ct, 0:CV_TAPS - 1], 0.0)
                V.memset(cpad[:, 0:SC_TAPS - 1], 0.0)
                norm(L, 0, lambda c: h[:, c, :], T, "mix_g", xlo, xhi)

                def cv(ct):
                    dve.wait_ge(cv_sig, L * SB_TILES + ct + 1)
                    TT(upad[:, ct, 30:30 + T], ps[:, (2 * ct) % 4, :], xf[:, ct % 2, :], ALU.mult).then_inc(cv_u, 1)

                def taps(ct, lo, hi):
                    for k in range(lo, hi):
                        drain()
                        w = pc("cw", ct * CV_TAPS + k)
                        if k == 0:
                            ins = TS(conv[:, ct, :], upad[:, ct, 0:T], w, pc("cb", ct), ALU.mult, ALU.add)
                        else:
                            ins = STT(out=conv[:, ct, :], in0=upad[:, ct, k:k + T], scalar=w, in1=conv[:, ct, :], op0=ALU.mult, op1=ALU.add)
                    if hi == CV_TAPS:
                        ins.then_inc(conv_ready, 1)

                def sc(ct):
                    b0, x0 = 8 + 3 * ct, 8 + 3 * ct + 2
                    dve.wait_ge(sc_copied, L * SB_TILES + ct + 1)
                    panel(x0 % 4, L, 3 + x0 // 4)
                    TT(cpad[:, 2:2 + T], ps[:, x0 % 4, :], sc_c[:, :], ALU.mult).then_inc(sc_cx, 1)
                    drain()
                    TS(sc_o[:, :], cpad[:, 0:T], pc("scw", ct * SC_TAPS), None, ALU.mult)
                    for k in range(1, SC_TAPS):
                        drain()
                        STT(out=sc_o[:, :], in0=cpad[:, k:k + T], scalar=pc("scw", ct * SC_TAPS + k), in1=sc_o[:, :], op0=ALU.mult, op1=ALU.add)
                    drain()
                    TT(yt[:, ct % 2, :], ps[:, b0 % 4, :], sc_o[:, :], ALU.mult).then_inc(sc_y, 1)

                def sc_lo(ct):
                    dve.wait_ge(shi_ready, L * SB_TILES + ct + 1)
                    TT(blo[:, 8 + ct, :], yt[:, ct % 2, :], bhi[:, 8 + ct, :].bitcast(F32), ALU.subtract).then_inc(slo_ready, 1)

                for hd in range(SB_HEADS):
                    dve.wait_ge(ln_ready, L * SB_HEADS + hd + 1)
                    STT(out=sp[:, :], in0=zps[:, 0:ZCOLS], scalar=0.0, in1=soft[:, :], op0=ALU.max, op1=ALU.add).then_inc(sp_ready, 1)
                    if hd >= 1:
                        taps((hd - 1) // 2, *((0, 16) if (hd - 1) % 2 == 0 else (16, CV_TAPS)))
                    if hd < 4:
                        cv(hd)
                    if hd >= 6:
                        sc_lo(hd - 6)
                    if hd >= 5:
                        drain()
                        sc(hd - 5)
                    if hd % 2:
                        dve.wait_ge(yhi_ready, L * SB_TILES + hd // 2 + 1)
                        TT(blo[:, hd // 2, :], ps[:, 7, :], bhi[:, hd // 2, :].bitcast(F32), ALU.subtract).then_inc(ylo_ready, 1)
                taps(3, 16, CV_TAPS)
                sc_lo(2)
                drain()
                sc(3)
                sc_lo(3)
                dve.wait_ge(mu_done, L + 1)
                for ct in range(SB_TILES):
                    STT(out=conv[:, ct, :], in0=ps[:, 6, :], scalar=-1.0 / (SB_TILES * P), in1=conv[:, ct, :],
                        op0=ALU.mult, op1=ALU.add).then_inc(dev_ready, 1)
                dve.wait_ge(ln_std, L + 1)
                V.reciprocal(std[:, :], std[:, :])
                drain()
                for ct in range(SB_TILES):
                    TT(conv[:, ct, :], conv[:, ct, :], std[:, :], ALU.mult).then_inc(ln_scaled, 1)
                for ct in range(SB_TILES):
                    dve.wait_ge(chi_ready, L * SB_TILES + ct + 1)
                    TT(blo[:, 4 + ct, :], conv[:, ct, :], bhi[:, 4 + ct, :].bitcast(F32), ALU.subtract).then_inc(clo_ready, 1)
                drain()
                with dve.Fori(0, KC) as dt:
                    for b in range(3):
                        dve.wait_ge(gate_sig, (L * KC + dt) * 3 + (b + 1))
                        if b < 2:
                            dve.wait_ge(br_done, (L * KC + dt) * 2 + (b + 1))
                        else:
                            dve.wait_ge(used[3], L * USED[3] + dt + (FRONT // 4 + 1))
                        TT(sg[:, b, :], ps[:, 3 + b, :], sg[:, b, :], ALU.mult).then_inc(br_used, 1)
                        if b:
                            drain()
                            TT(sg[:, 0, :], sg[:, 0, :], sg[:, b, :], ALU.add)
                    drain()
                    V.tensor_copy(mghi[:, dt, :], sg[:, 0, :])
                    drain()
                    TT(mglo[:, dt, :], sg[:, 0, :], mghi[:, dt, :].bitcast(F32), ALU.subtract).then_inc(mlo_ready, 1)
                drain()

                def residual(use):
                    for i in range(KC):
                        panel(i % 4, L, use + i // 4)
                        TT(h[:, i, :], h[:, i, :], ps[:, i % 4, :], ALU.add).then_inc(h_ready, 1)

                residual(FRONT // 4 + KC)
                norm(L, 1, lambda c: mem[:, c, :], N_MEM, "mem_g", mlo, mhi)
                norm(L, 2, lambda c: h[:, c, :], T, "xa_g", xlo, xhi)
                for hd in range(XA_HEADS):
                    k, a = 2 * (hd % 2), 8 + 4 * (hd % 2)
                    dve.wait_ge(xs_done, L * XA_HEADS + hd + 1)
                    V.tensor_reduce(small[:, a + 16:a + 20], ps[:, k:k + 2, :].rearrange("p a (b m) -> p (a b) m", b=2), AX.X, ALU.max)
                    drain()
                    TS(small[:, a:a + 4], small[:, a + 16:a + 20], -1.0, None, ALU.mult).then_inc(xs_neg, 1)
                    dve.wait_ge(xs_exp, (L * XA_HEADS + hd + 1) * TB)
                    V.reciprocal(small[:, a + 24:a + 28], small[:, a + 8:a + 12])
                    drain()
                    for tb in range(TB):
                        TS(prob[:, hd % 2, tb * N_MEM:(tb + 1) * N_MEM], prob[:, hd % 2, tb * N_MEM:(tb + 1) * N_MEM],
                           small[:, a + 24 + tb:a + 25 + tb], None, ALU.mult).then_inc(xs_norm, 1)
                    for c in range(2):
                        dve.wait_ge(xohi_ready, L * KC + hd * 2 + c + 1)
                        TT(olo[:, 2 * hd + c, :], ps[:, 6 + c, :], ohi[:, 2 * hd + c, :].bitcast(F32), ALU.subtract).then_inc(xolo_ready, 1)
                residual(FRONT // 4 + KC + 8)
                norm(L, 3, lambda c: h[:, c, :], T, "ffn_g", xlo, xhi)
                for l in range(LISTS):
                    hold(score_done, L * LISTS + l + 1)
                    scores = [ps[:, 4 + l % 4, tb * NK:(tb + 1) * NK] for tb in range(TB)]
                    for tb in range(TB):
                        V.max(vals[:, tb, l, 0:8], scores[tb])
                    drain()
                    for tb in range(TB):
                        V.match_replace(rest[:, tb, :], vals[:, tb, l, 0:8], scores[tb], NEG)
                    for tb in range(TB):
                        V.max_index(inds[:, tb, l, 0:8], vals[:, tb, l, 0:8], scores[tb]).then_inc(score_used, 1)
                    drain()
                    for tb in range(TB):
                        V.max(vals[:, tb, l, 8:16], rest[:, tb, :])
                    drain()
                    for tb in range(TB):
                        V.max_index(inds[:, tb, l, 8:16], vals[:, tb, l, 8:16], rest[:, tb, :])
                    drain()
                with dve.Fori(0, TB) as b:
                    v4 = vals[:, b, :, :].rearrange("p (h q) k -> p h q k", q=2)
                    i4 = inds[:, b, :, :].rearrange("p (h q) k -> p h q k", q=2)
                    dve.wait_ge(rows_free, (L * TB + b) * P + HROWS)
                    TT(cand[:, :, :].rearrange("p h (i j) -> p h i j", i=TOPK),
                       v4[:, :, 0, :].unsqueeze(3).to_broadcast([P, PH, TOPK, TOPK]),
                       v4[:, :, 1, :].unsqueeze(2).to_broadcast([P, PH, TOPK, TOPK]), ALU.add)
                    drain()
                    first = [slice(hd * TOPK, hd * TOPK + 8) for hd in range(PH)]
                    second = [slice(hd * TOPK + 8, (hd + 1) * TOPK) for hd in range(PH)]
                    for hd in range(PH):
                        V.max(picks[:, first[hd]], cand[:, hd, :])
                    drain()
                    for hd in range(PH):
                        V.max_index(pick_i[:, first[hd]], picks[:, first[hd]], cand[:, hd, :])
                    drain()
                    for hd in range(PH):
                        V.match_replace(cand[:, hd, :], picks[:, first[hd]], cand[:, hd, :], NEG)
                    drain()
                    for hd in range(PH):
                        V.max(picks[:, second[hd]], cand[:, hd, :])
                    drain()
                    for hd in range(PH):
                        V.max_index(pick_i[:, second[hd]], picks[:, second[hd]], cand[:, hd, :])
                    p3 = picks[:, :].rearrange("p (h k) -> p h k", k=TOPK)
                    V.tensor_copy(small[:, 40:48], p3[:, :, 0])
                    drain()
                    TT(p3, p3, small[:, 40:48].unsqueeze(2).to_broadcast([P, PH, TOPK]), ALU.subtract).then_inc(pick_diff, 1)
                    TS(rank[:, 0, :], pick_i[:, :], 4, None, ALU.logical_shift_right)
                    TS(rank[:, 1, :], pick_i[:, :], TOPK - 1, None, ALU.bitwise_and)
                    l4 = lookup[:, :, :].rearrange("p (h k) j -> p h k j", h=PH)
                    for q in range(2):
                        drain()
                        TT(lookup[:, :, :], rank[:, q, :].unsqueeze(2).to_broadcast([P, SEL, TOPK]),
                           cst("iota16", TOPK).unsqueeze(1).to_broadcast([P, SEL, TOPK]), ALU.is_equal)
                        drain()
                        TT(l4, l4, i4[:, :, q, :].unsqueeze(2).to_broadcast([P, PH, TOPK, TOPK]), ALU.mult)
                        drain()
                        V.tensor_reduce(eidx[:, q, :], lookup[:, :, :], AX.X, ALU.add)
                    dve.wait_ge(pick_exp, L * TB + b + 1)
                    V.tensor_reduce(small[:, 48:56], p3, AX.X, ALU.add)
                    drain()
                    V.reciprocal(small[:, 40:48], small[:, 48:56])
                    drain()
                    TT(eidx[:, 2, :].rearrange("p (h k) -> p h k", k=TOPK), p3,
                       small[:, 40:48].unsqueeze(2).to_broadcast([P, PH, TOPK]), ALU.mult).then_inc(pick_ready, 1)
                    dve.wait_ge(selT_ready, L * TB + b + 1)
                    dve.nop(nofuse=True)
                    with dve.Fori(0, P // HROWS) as g:
                        for k in range(HROWS):
                            t = dve.snap(g * HROWS + k)
                            dve.wait_ge(rows_free, (L * TB + b) * P + g * HROWS + (k + 1))
                            TS(onehot2[:, k, :], cst("iota"), selT[:, 1, bass.ds(t, 1)], None, ALU.is_equal)
                            TS(onehot1[:, k, :], cst("iota"), selT[:, 0, bass.ds(t, 1)], selT[:, 2, bass.ds(t, 1)],
                               ALU.is_equal, ALU.mult).then_inc(rows_ready, 1)

                def weigh(j, r):
                    k, n = r % 2, L * PAIRS + j * RV + r
                    drain()
                    dve.wait_ge(gt_loaded[k], (L * (PAIRS // 2) + j * (RV // 2) + (r // 2 + 1)) * 16)
                    if k == 0:
                        dve.wait_ge(act_loaded[0], (L * (PAIRS // 2) + j * (RV // 2) + (r // 2 + 1)) * 16)
                    elif r % 4 == 1:
                        dve.wait_ge(act_loaded[1], (L * (PAIRS // 4) + j * (RV // 4) + (r // 4 + 1)) * 16)
                    for m in range(2):
                        if r % 4 == 3:
                            dve.wait_ge(gelu_ready, (L * NROUNDS + j) * (2 * RU) + (r // 4 * 2 + m + 1))
                        dve.wait_ge(eh_ready, n * 2)
                        TT(weighted[:, m, :], act_e[:, k, m, :], gtile[:, k, m, :], ALU.mult).then_inc(w_ready, 1)
                    for m in range(2):
                        dve.wait_ge(eh_ready, n * 2 + (m + 1))
                        TT(el[:, k, m, :], weighted[:, m, :], eh[:, k, m, :].bitcast(F32), ALU.subtract).then_inc(el_ready, 1)

                def gather(n):
                    for c in range(KC):
                        dve.wait_ge(v_done, (L * PAIRS + n) * KC + (c + 1))
                        TT(h[:, c, :], h[:, c, :], ps[:, 2 + c % 6, :], ALU.add).then_inc(acc_done, 1)

                hold(g_stored, (L + 1) * (TB * 16 * PIECES))
                weigh(L * 0, 0)
                with dve.Fori(0, NROUNDS - 1) as j:
                    for r in range(RV):
                        weigh(*((j, r + 1) if r + 1 < RV else (j + 1, 0)))
                        gather(j * RV + r)
                for r in range(RV):
                    if r + 1 < RV:
                        weigh(L * 0 + (NROUNDS - 1), r + 1)
                    gather(L * 0 + (PAIRS - RV + r))
            dve.wait_ge(std_ready, LAYERS * 4 + 1)
            V.reciprocal(std[:, :], std[:, :])
            drain()
            for c in range(KC):
                STT(out=h[:, c, :], in0=h[:, c, :], scalar=pc("fin_g", c), in1=std[:, :], op0=ALU.mult, op1=ALU.mult).then_inc(out_ready, 1)

        @block.tensor
        def _(pe):
            MM, TR = nc.tensor.matmul, nc.tensor.transpose

            def linear(s, L, use, out, ahi, alo, chunks=range(KC), w0=0, done=None):
                pe.wait_ge(split[s], L * SPLITS[s] + use + 1)
                for i, c in enumerate(chunks):
                    a = SLOT[s] + (w0 + i) * P
                    for n, (w, x) in enumerate(((whi, ahi), (whi, alo), (wlo, ahi))):
                        ins = MM(out, w[:, a:a + P], x[:, c, :], start=(i == 0 and n == 0), stop=(i == len(chunks) - 1 and n == 2))
                ins.then_inc(used[s] if done is None else done, 1)

            def norm(L, k, w):
                for c in range(KC):
                    pe.wait_ge(sq_ready, L * NORMS + k * KC + c + 1)
                    MM(ps[:, 7, 0:w], cst("ones"), sq[:, c % 2, 0:w], start=(c == 0), stop=(c == KC - 1)).then_inc(sq_used, 1)

            pe.wait_ge(consts_ready, 4)
            pe.nop(nofuse=True)
            with pe.Fori(0, LAYERS) as L:
                pe.wait_ge(acc_done, L * ACC)
                norm(L, 0, T)
                pe.wait_ge(xlo_ready, L * NORMS + KC)
                pe.nop(nofuse=True)
                with pe.Fori(0, 3) as i:
                    for s in range(4):
                        pe.wait_ge(qkv_copied, L * 12 + i * 4)
                        linear(s, L, i, ps[:, s, :], xhi, xlo)
                pe.wait_ge(qkv_copied, (L + 1) * 12)
                for b in range(TB):
                    for t in range(SB_TILES):
                        ins = TR(ps[:, 4 + b, t * P:(t + 1) * P], vT[:, t, b * P:(b + 1) * P], cst("ident"))
                    ins.then_inc(vt_done, 1)
                pe.wait_ge(vt_copied, (L + 1) * TB)

                def front(n):
                    if 4 <= n < 8:
                        pe.wait_ge(cv_u, L * SB_TILES + n // 2 - 1)
                    elif 8 <= n < 12:
                        pe.wait_ge(cv_u, L * SB_TILES + (4 if n >= 10 else 3))
                    elif n >= 12:
                        tile, which = divmod(n - 12, 3)
                        pe.wait_ge((sc_y, sc_copied, sc_cx)[which], L * SB_TILES + tile + 1)
                    linear(n % 4, L, 3 + n // 4, ps[:, n % 4, :], xhi, xlo)

                for hd in range(SB_HEADS):
                    r, tile = 64 * (hd % 2), hd // 2
                    pe.wait_ge(a_ready, L * SB_HEADS + hd)
                    for sb in range(TB):
                        z = zps[:, ZO[sb]:ZO[sb] + ZW[sb]]
                        MM(z, kT[r:r + 64, tile, sb * P:(sb + 1) * P], qT[r:r + 64, tile, sb * P:T], start=(sb != 3), stop=False, skip_group_check=True)
                        ins = MM(z[:, 0:P], identb[:, :], negmaskb[:, :], start=False, stop=False, skip_group_check=True)
                    ins.then_inc(z_done, 1)
                    front(2 * hd)
                    pe.wait_ge(sp_ready, L * SB_HEADS + hd + 1)
                    for sb in range(TB - 1, -1, -1):
                        z = zps[:, ZO[sb]:ZO[sb] + ZW[sb]]
                        for sj in range(sb + 1, TB):
                            MM(z[:, ZW[sb] - ZW[sj]:], cst("negones"), sp[:, ZO[sj]:ZO[sj] + ZW[sj]], start=False, stop=False, skip_group_check=True)
                        ins = MM(z, cst("tri"), sp[:, ZO[sb]:ZO[sb] + ZW[sb]], start=False, stop=True, skip_group_check=True)
                    ins.then_inc(c_done, 1)
                    front(2 * hd + 1)
                    pe.wait_ge(a_ready, L * SB_HEADS + hd + 1)
                    pe.wait_ge(ylo_ready, L * SB_TILES + tile)
                    for sb in range(TB):
                        ins = MM(ps[r:r + 64, 7, sb * P:T], vtok[:, sb, hd * 64:(hd + 1) * 64], soft[:, ZO[sb]:ZO[sb] + ZW[sb]],
                                 start=(sb == 0), stop=(sb == TB - 1), skip_group_check=True)
                    ins.then_inc(y_done, 1)
                for n in range(16, 20):
                    front(n)
                pe.wait_ge(conv_ready, (L + 1) * SB_TILES)
                for ct in range(SB_TILES):
                    ins = MM(ps[:, 6, :], cst("ones"), conv[:, ct, :], start=(ct == 0), stop=(ct == SB_TILES - 1))
                ins.then_inc(mu_done, 1)
                pe.wait_ge(ylo_ready, (L + 1) * SB_TILES)
                for ct in range(SB_TILES):
                    pe.wait_ge(dsq_ready, L * SB_TILES + ct + 1)
                    MM(ps[:, 7, :], cst("ones"), sq[:, ct % 2, :], start=(ct == 0), stop=(ct == SB_TILES - 1)).then_inc(var_done, 1)
                pe.wait_ge(slo_ready, (L + 1) * SB_TILES)
                pe.nop(nofuse=True)
                with pe.Fori(0, KC) as dt:
                    pe.wait_ge(gate_sig, (L * KC + dt) * 3)
                    for b in range(3):
                        linear(b, L, dt + FRONT // 4, ps[:, b, :], xhi, xlo)
                    pe.wait_ge(clo_ready, (L + 1) * SB_TILES)
                    pe.wait_ge(br_used, (L * KC + dt) * 3)
                    for b in range(3):
                        linear(3, L, dt + FRONT // 4, ps[:, 3 + b, :], bhi, blo, range(4 * b, 4 * b + 4), 4 * b, None if b == 2 else br_done)
                pe.wait_ge(mlo_ready, (L + 1) * KC)
                for i in range(2):
                    for s in range(4):
                        pe.wait_ge(h_ready, L * ROUNDS + i * 4)
                        linear(s, L, FRONT // 4 + KC + i, ps[:, s, :], mghi, mglo)
                    if i == 0:
                        norm(L, 1, N_MEM)
                pe.wait_ge(h_ready, L * ROUNDS + KC)
                pe.wait_ge(xlo_ready, L * NORMS + 2 * KC)
                for i in range(16):
                    if i == 4:
                        pe.wait_ge(std_ready, L * 4 + 2)
                        norm(L, 2, T)
                    if i >= 8:
                        pe.wait_ge(kv_copied, L * 16 + i - 7)
                    linear(i % 4, L, G1 + 2 + i // 4, ps[:, i % 4, kv_cols(i)], mhi, mlo)
                pe.wait_ge(kv_copied, (L + 1) * 16)
                pe.wait_ge(std_ready, L * 4 + 3)
                for m in range(MB):
                    for c in range(KC):
                        ins = TR(ps[:, 4 + 2 * m + c // 4, (c % 4) * P:(c % 4 + 1) * P], xvT[:, c, m * P:(m + 1) * P], cst("ident"))
                    ins.then_inc(xvt_done, 1)
                pe.wait_ge(xlo_ready, L * NORMS + 3 * KC)
                pe.nop(nofuse=True)
                with pe.Fori(0, 2) as i:
                    for s in range(4):
                        pe.wait_ge(xq_copied, L * 8 + i * 4)
                        linear(s, L, i + (FRONT // 4 + KC + 6), ps[:, s, :], xhi, xlo)
                pe.wait_ge(xq_copied, (L + 1) * 8)
                pe.wait_ge(xvt_copied, (L + 1) * MB)

                def xa_scores(hd):
                    k = 2 * (hd % 2)
                    for tb in range(TB):
                        for c in range(2):
                            ins = MM(ps[:, k + tb // 2, (tb % 2) * N_MEM:(tb % 2 + 1) * N_MEM],
                                     xqT[:, 2 * hd + c, tb * P:(tb + 1) * P], xkT[:, 2 * hd + c, :], start=(c == 0), stop=(c == 1))
                    ins.then_inc(xs_done, 1)

                xa_scores(0)
                for hd in range(XA_HEADS):
                    if hd + 1 < XA_HEADS:
                        pe.wait_ge(xs_exp, (L * XA_HEADS + hd) * TB)
                        xa_scores(hd + 1)
                    pe.wait_ge(xs_norm, (L * XA_HEADS + hd + 1) * TB)
                    pe.wait_ge(xt_copied, L * (XA_HEADS * MB) + hd * MB)
                    for m in range(MB):
                        for tb in range(TB):
                            a = tb * N_MEM + m * P
                            ins = TR(ps[:, 4 + m, tb * P:(tb + 1) * P], prob[:, hd % 2, a:a + P], cst("ident"))
                        ins.then_inc(xt_done, 1)
                    pe.wait_ge(xt_copied, L * (XA_HEADS * MB) + (hd + 1) * MB)
                    pe.wait_ge(xolo_ready, L * KC + 2 * hd)
                    for c in range(2):
                        for m in range(MB):
                            ins = MM(ps[:, 6 + c, :], xv[:, m, (2 * hd + c) * P:(2 * hd + c + 1) * P], probT[:, m, :], start=(m == 0), stop=(m == MB - 1))
                        ins.then_inc(xo_done, 1)
                pe.wait_ge(xolo_ready, (L + 1) * KC)
                pe.wait_ge(xs_exp, (L + 1) * (XA_HEADS * TB))
                pe.nop(nofuse=True)
                with pe.Fori(0, 2) as i:
                    for s in range(4):
                        pe.wait_ge(h_ready, L * ROUNDS + i * 4 + KC)
                        linear(s, L, i + (FRONT // 4 + KC + 8), ps[:, s, :], ohi, olo)
                norm(L, 3, T)
                pe.wait_ge(h_ready, (L + 1) * ROUNDS)
                pe.wait_ge(std_ready, L * 4 + 4)
                pe.wait_ge(xlo_ready, L * NORMS + 4 * KC)
                pe.wait_ge(keys_loaded, (L + 1) * 16)

                def query(l):
                    if l >= 4:
                        pe.wait_ge(pq_copied, L * LISTS + l - 3)
                    linear(l % 4, L, FRONT // 4 + KC + 10 + l // 4, ps[:, l % 4, :], xhi, xlo)

                def score(l):
                    pe.wait_ge(pq_copied, L * LISTS + l + 1)
                    if l >= 4:
                        pe.wait_ge(score_used, (L * LISTS + l - 3) * TB)
                    for tb in range(TB):
                        ins = MM(ps[:, 4 + l % 4, tb * NK:(tb + 1) * NK], pqT[:, l % 2, tb * P:(tb + 1) * P], keys[:, l, :], start=True, stop=True)
                    ins.then_inc(score_done, 1)

                query(0)
                for l in range(1, LISTS):
                    query(l)
                    score(l - 1)
                score(LISTS - 1)
                def early_panel(s, i):
                    pe.wait_ge(early_ready[s], L * EARLY + i)
                    linear(s, L, i + FIRST, ps[:, 5 + s, :], xhi, xlo)

                def turn(b):
                    pe.wait_ge(pick_ready, L * TB + b + 1)
                    for q in range(3):
                        ins = TR(ps[:, 4, q * P:(q + 1) * P], eidx[:, q, :], cst("ident"))
                    ins.then_inc(selT_done, 1)

                pe.wait_ge(score_used, (L + 1) * (LISTS * TB))
                pe.nop(nofuse=True)
                with pe.Fori(0, LEAD) as i:
                    for s in range(2):
                        early_panel(s, i)
                turn(L * 0)

                def rows(b):
                    with pe.Fori(0, WITH) as g:
                        for s in range(2):
                            early_panel(s, b * (WITH + BEHIND) + g + LEAD)
                            for k in range(8 * s, 8 * s + 8):
                                if k % 8 == 0:
                                    pe.wait_ge(g_copied, (L * TB + b) * (P // 4) + g * 4)
                                pe.wait_ge(rows_ready, (L * TB + b) * P + g * 16 + (k + 1))
                                MM(ps[:, k // 4, (k % 4) * NK:(k % 4 + 1) * NK], onehot2[:, k % HROWS, :], onehot1[:, k % HROWS, :],
                                   start=True, stop=True).then_inc(rows_free, 1)
                    for i in range(BEHIND):
                        for s in range(2):
                            early_panel(s, b * (WITH + BEHIND) + (LEAD + WITH + i))

                with pe.Fori(0, TB - 1) as b:
                    rows(b)
                    turn(b + 1)
                rows(L * 0 + (TB - 1))
                pe.wait_ge(g_copied, (L + 1) * (TB * P // 4))
                for s in range(2):
                    pe.wait_ge(early_ready[s], (L + 1) * EARLY)
                pe.nop(nofuse=True)

                def up(j, r, pair, use):
                    pe.wait_ge(gelu_ready, (L * NROUNDS + j) * (2 * RU) + r // 4 * 2)
                    for m in range(2):
                        linear(pair + m, L, use, ps[:, m, :], xhi, xlo)

                def down(j, r, pair, use):
                    n = L * PAIRS + j * RV + r
                    pe.wait_ge(el_ready, n * 2 + 2)
                    for m in range(2):
                        pe.wait_ge(split[pair + m], L * SPLITS[pair] + use + 1)
                    for c in range(KC):
                        if c == 0:
                            pe.wait_ge(acc_done, n * KC)
                        if c >= 6:
                            pe.wait_ge(acc_done, n * KC + (c - 5))
                        for m in range(2):
                            a = SLOT[pair + m] + c * P
                            for q, (w, x) in enumerate(((whi, eh), (whi, el), (wlo, eh))):
                                ins = MM(ps[:, 2 + c % 6, :], w[:, a:a + P], x[:, r % 2, m, :], start=(m == 0 and q == 0), stop=(m == 1 and q == 2))
                        ins.then_inc(v_done, 1)

                with pe.Fori(0, NROUNDS) as j:
                    r = 0
                    for step, what in enumerate(ROUND):
                        pair = 2 * (step % 2)
                        use = j * (len(ROUND) // 2) + (FIRST + (0 if pair else EARLY) + step // 2)
                        if what == "u":
                            up(j, r + 1, pair, use)
                        else:
                            down(j, r, pair, use)
                            r += 1
            norm(LAYERS, 0, T)


def kernel(**inputs):
    import numpy as np
    import concourse.bacc as bacc
    from concourse.bass_utils import run_bass_kernel_spmd

    a = {k: np.ascontiguousarray(v) for k, v in inputs.items()}

    def rows(w):
        lead, (K, N) = w.shape[:-2], w.shape[-2:]
        w = w.reshape(*lead, K // P, P, N // P, P)
        n = len(lead)
        return np.ascontiguousarray(w.transpose(*range(n), n + 2, n + 1, n, n + 3)).reshape(*lead, N // P, P, K)

    def cols(v):
        return v.reshape(LAYERS, -1, P).transpose(0, 2, 1)

    w_in = rows(a["w_in"])
    cv, sc, gate = w_in[:, 12:20], w_in[:, 20:32], w_in[:, 32:56]
    cv = cv[:, [0, 4, 1, 5, 2, 6, 3, 7]]
    sc = sc[:, [0, 4, 8, 1, 5, 9, 2, 6, 10, 3, 7, 11]]
    gate = gate[:, [b * KC + dt for dt in range(KC) for b in range(3)]]
    branch = rows(a["w_branch"]).transpose(0, 2, 3, 1, 4)
    par = np.concatenate([
        cols(a["norm_mix_g"]), cols(a["norm_xa_g"]), cols(a["norm_mem_g"]), cols(a["norm_ffn_g"]),
        a["conv_dw_w"].reshape(LAYERS, CV_TAPS, SB_TILES, P).transpose(0, 3, 2, 1).reshape(LAYERS, P, -1),
        cols(a["conv_dw_b"]), cols(a["conv_ln_g"]), cols(a["conv_ln_b"]),
        a["sc_w"].reshape(LAYERS, SC_TAPS, SB_TILES, P).transpose(0, 3, 2, 1).reshape(LAYERS, P, -1),
        cols(a["b_gate"]), np.stack([a["final_g"].reshape(KC, P).T] * LAYERS)], axis=2)
    i = np.arange(P, dtype=np.float32)
    low = (i[:, None] >= i[None, :]).astype(np.float32)
    const = np.concatenate([
        np.eye(P, dtype=np.float32), np.ones((P, P), np.float32), -np.ones((P, P), np.float32),
        -low, np.tile(i, (P, 1)), low * np.float32(-1e30), np.tile(i[:TOPK], (P, 1))], axis=1)
    L = LAYERS
    order = [(0, n) for n in range(2 * EARLY)]
    for j in range(NROUNDS):
        r = 0
        for what in ROUND:
            q = r + (what == "u")
            n = 2 * EARLY + 4 * j + q // 4 * 2 if q % 4 == 3 else 12 * j + q // 4 * 6 + q % 4 * 2
            order += [(int(what == "v"), n), (int(what == "v"), n + 1)]
            r += what == "v"
    u_v = rows(a["peer_u"].transpose(0, 2, 1)), a["peer_v"].reshape(L, NK, P, D)
    experts = np.stack([u_v[which][:, n] for which, n in order], axis=1)
    data = {
        "xT": a["x"][0].T.reshape(KC, P, T).transpose(1, 0, 2),
        "memT": a["mem"][0].T.reshape(KC, P, N_MEM).transpose(1, 0, 2),
        "par": par,
        "const": const,
        "front": np.concatenate([w_in[:, 0:12], cv, sc], axis=1).reshape(L * FRONT, P, D),
        "gates": gate.reshape(L * GATES, P, D),
        "branch": branch.reshape(L * KC, P, 12 * P),
        "back": np.concatenate([rows(a[n]) for n in ("w_out", "xa_wkv", "xa_wq", "xa_wo", "peer_wq")], axis=1).reshape(L * BACK, P, D),
        "keys": a["peer_keys"].reshape(L, LISTS, NK, P).transpose(0, 3, 1, 2),
        "experts": experts.reshape(L * STREAM, P, D),
    }
    nc = bacc.Bacc("TRN2", target_bir_lowering=False, num_devices=1)
    arrays, args = {}, []
    for name, v in data.items():
        v = np.ascontiguousarray(v)
        arrays[f"in_{name}"] = v
        args.append(nc.dram_tensor(f"in_{name}", v.shape, mybir.dt.from_np(v.dtype), kind="ExternalInput").ap())
    out = nc.dram_tensor("out", (P, KC, T), F32, kind="ExternalOutput").ap()
    build_trunk(nc, *args, out)
    r = run_bass_kernel_spmd(nc, [arrays], core_ids=[0])
    return r.results[0]["out"].transpose(2, 1, 0).reshape(1, T, D)
```

```python
from contextlib import ExitStack

import concourse.bass as bass
from concourse import mybir

P = 128
T = 512
D = 1024
KC = D // P
LAYERS = 2
TB = T // P
N_MEM = 256
MB = N_MEM // P
SB_TILES = 4
SB_HEADS = 8
CV_TAPS = 31
SC_TAPS = 3
XA_HEADS = 4
XA_DH = D // XA_HEADS
PH = 8
LISTS = 2 * PH
NK = 128
TOPK = 16
SEL = PH * TOPK
NEG = -3.0e38

PAR, PAR_COLS = {}, 0
for _n, _c in (("mix_g", KC), ("xa_g", KC), ("mem_g", KC), ("ffn_g", KC), ("cw", SB_TILES * CV_TAPS),
               ("cb", SB_TILES), ("lng", SB_TILES), ("lnb", SB_TILES), ("scw", SB_TILES * SC_TAPS),
               ("bg", 3 * KC), ("fin_g", KC)):
    PAR[_n] = PAR_COLS
    PAR_COLS += _c

FRONT = 12 + 8 + 12
BACK = 8 + 16 + 8 + 8 + 16
GATES = 3 * KC
PAIRS = NK // 2
FIRST = FRONT // 4 + KC + BACK // 4
LEAD, WITH, BEHIND = 4, P // 16, 3
EARLY = LEAD + TB * (WITH + BEHIND)
ROUND = "uvvvvuvvvv"
RV, RU = ROUND.count("v"), ROUND.count("u")
NROUNDS = PAIRS // RV
assert EARLY == NROUNDS * (RV - RU) and len(ROUND) % 2 == 0
LATE = NROUNDS * len(ROUND) // 2
SPLITS = [FIRST + EARLY + LATE] * 2 + [FIRST + LATE] * 2
USED = [FIRST + EARLY + NROUNDS] * 2 + [FIRST + NROUNDS] * 2
G1 = FRONT // 4 + KC
ROUNDED = [KC - 1 + 8 + n - FIRST for n in SPLITS[:3]] + [8 + SPLITS[3] - FIRST]
STREAM = 2 * (EARLY + PAIRS + NROUNDS * RU)
HB = P // 2
PARTS = (0, 48, 96, NK)
PIECES = len(PARTS) - 1
HROWS = 16
ROUNDS = 2 * KC

F32 = mybir.dt.float32
F32R = mybir.dt.float32r
BF16 = mybir.dt.bfloat16
U32 = mybir.dt.uint32
ACT = mybir.ActivationFunctionType
ALU = mybir.AluOpType
AX = mybir.AxisListType

ZW = [T - P * sb for sb in range(TB)]
ZO = [0, 512, 1024, 896]
ZCOLS = sum(ZW)
CONSTS = ("ident", "ones", "negones", "tri", "iota", "negmask", "iota16")


def build_trunk(nc, xT, memT, par_d, const_d, front_d, gates_d, branch_d, back_d, keys_d, expert_d, outT):
    gate_d = nc.dram_tensor("gate_table", (2 * TB, P, NK, HB), F32, kind="Internal").ap()
    early_d = nc.dram_tensor("early_gelu", (2 * EARLY, P, T), F32, kind="Internal").ap()
    ctx = ExitStack()
    with ctx:
        def sem(name):
            return ctx.enter_context(nc.semaphore(name))

        top = [(nc.sbuf_base + 63) // 64 * 64]

        def region(size):
            at = top[0]
            top[0] += (size + 31) // 32 * 32
            return at

        def place(name, at, shape, dt):
            return nc.alloc_sbuf_tensor_at(name, [P] + list(shape), dt, offset=at)

        SLOT = [0, 1024, 2048, 3072]
        RING = 3 * 1024 + 1536
        RAW = region(RING * 4)
        raw = place("raw", RAW, [RING], F32)
        early = place("early", RAW + SLOT[2] * 4, [2, T], F32)
        WHI, WLO = region(RING * 4), region(RING * 4)
        whi = place("whi", WHI, [RING], F32R)
        wlo = place("wlo", WLO, [RING], F32R)
        cand = place("cand", WHI + SLOT[2] * 4, [PH, TOPK * TOPK], F32)
        onehot2 = place("onehot2", WLO + SLOT[2] * 4, [HROWS, NK], F32)
        selT = place("selT", WLO + SLOT[2] * 4 + HROWS * NK * 4, [3, P], F32)
        h = place("h", region(KC * T * 4), [KC, T], F32)
        xhi = place("xhi", region(KC * T * 4), [KC, T], F32R)
        xlo = place("xlo", region(KC * T * 4), [KC, T], F32R)
        E = region(24 * T * 4)
        bhi = place("bhi", E, [12, T], F32R)
        blo = place("blo", E + 12 * T * 4, [12, T], F32R)
        sp = place("sp", E + 4 * T * 4, [ZCOLS], F32)
        soft = place("soft", E + 16 * T * 4, [ZCOLS], F32)
        mhi = place("mhi", E + 8192, [KC, N_MEM], F32R)
        mlo = place("mlo", E + 16384, [KC, N_MEM], F32R)
        xvT = place("xvT", E + 24576, [KC, N_MEM], F32)
        xkT = place("xkT", E + 32768, [KC, N_MEM], F32)
        xv = place("xv", E + 40960, [MB, D], F32)
        ohi = place("ohi", E, [KC, T], F32R)
        olo = place("olo", E + 16384, [KC, T], F32R)
        F = region(16 * T * 4)
        qT = place("qT", F, [SB_TILES, T], F32)
        kT = place("kT", F + 8192, [SB_TILES, T], F32)
        vT = place("vT", F + 16384, [SB_TILES, T], F32)
        conv = place("conv", F + 16384, [SB_TILES, T], F32)
        vtok = place("vtok", F + 24576, [TB, T], F32)
        sc_c = place("sc_c", F, [T], F32)
        sc_o = place("sc_o", F + 2048, [T], F32)
        yt = place("yt", F + 8192, [2, T], F32)
        mghi = place("mghi", F, [KC, T], F32R)
        mglo = place("mglo", F + 16384, [KC, T], F32R)
        xqT = place("xqT", F, [KC, T], F32)
        prob = place("prob", F + 16384, [2, TB * N_MEM], F32)
        probT = place("probT", F + 24576, [MB, T], F32)
        gbuf = place("gbuf", E, [2, NK, HB], F32)
        keys = place("keys", E + 65536, [LISTS, NK], F32)
        S = E + 65536 + 4096
        picks = place("picks", S, [SEL], F32)
        pick_i = place("pick_i", S + 512, [SEL], U32)
        rank = place("rank", S + 1024, [2, SEL], U32)
        eidx = place("eidx", S + 2048, [3, SEL], F32)
        vals = place("vals", E + 65536 + 8192, [TB, LISTS, TOPK], F32)
        inds = place("inds", E + 65536 + 12288, [TB, LISTS, TOPK], U32)
        act_e = place("act_e", E, [2, 2, T], F32)
        gtile = place("gtile", E + 8192, [2, 2 * TB, 2, HB], F32)
        eh = place("eh", E + 16384, [2, 2, T], F32R)
        el = place("el", E + 24576, [2, 2, T], F32R)
        weighted = place("weighted", E + 32768, [2, T], F32)
        const = place("const", region(6 * 512 + 64), [6 * P + TOPK], F32)
        identb = place("identb", region(256), [P], BF16)
        negmaskb = place("negmaskb", region(256), [P], BF16)
        par = place("par", region(PAR_COLS * 4), [PAR_COLS], F32)
        std = place("std", region(T * 4), [T], F32)
        SQ = region(4 * T * 4)
        sq = place("sq", SQ, [2, T], F32)
        xf = place("xf", SQ + 2 * T * 4, [2, T], F32)
        sg = place("sg", SQ, [3, T], F32)
        pqT = place("pqT", SQ, [2, T], F32)
        rest = place("rest", SQ + 2 * T * 4, [TB, NK], F32)
        UP = region(SB_TILES * (T + 30) * 4 + (T + 2) * 4)
        upad = place("upad", UP, [SB_TILES, T + 30], F32)
        cpad = place("cpad", UP + SB_TILES * (T + 30) * 4, [T + 2], F32)
        mem = place("mem", UP, [KC, N_MEM], F32)
        lookup = place("lookup", UP, [SEL, TOPK], F32)
        small = place("small", region(64 * 4), [64], F32)
        assert top[0] <= nc.sbuf_usable_end, (top[0], nc.sbuf_usable_end)
        onehot1 = place("onehot1", SQ, [HROWS, NK], F32)

        ps = ctx.enter_context(nc.psum_tensor("ps", [P, 8, T], F32))

        def down_bank(r, c):
            return 2 + (c + 2 * (r % 2)) % 6

        def cst(name, w=P):
            k = CONSTS.index(name) * P
            return const[:, k:k + w]

        def pc(name, k):
            k += PAR[name]
            return par[:, k:k + 1]

        loaded = [sem(f"loaded{s}") for s in range(4)]
        rounded = [sem(f"rounded{s}") for s in range(4)]
        split = [sem(f"split{s}") for s in range(4)]
        used = [sem(f"used{s}") for s in range(4)]
        x_loaded, par_loaded, const_loaded, mem_loaded, keys_loaded = (
            sem(n) for n in ("x_loaded", "par_loaded", "const_loaded", "mem_loaded", "keys_loaded"))
        consts_ready = sem("consts_ready")
        sq_ready, sq_used, std_ready, xf_ready, xhi_ready, xlo_ready = (
            sem(n) for n in ("sq_ready", "sq_used", "std_ready", "xf_ready", "xhi_ready", "xlo_ready"))
        h_ready = sem("h_ready")
        qkv_copied, vt_done, vt_copied = sem("qkv_copied"), sem("vt_done"), sem("vt_copied")
        z_done, ln_ready, sp_ready, c_done, a_ready, y_done = (
            sem(n) for n in ("z_done", "ln_ready", "sp_ready", "c_done", "a_ready", "y_done"))
        yhi_ready, ylo_ready = sem("yhi_ready"), sem("ylo_ready")
        cv_sig, cv_u, conv_ready = sem("cv_sig"), sem("cv_u"), sem("conv_ready")
        mu_done, dev_ready, dsq_ready, var_done, ln_std, ln_scaled, chi_ready, clo_ready = (
            sem(n) for n in ("mu_done", "dev_ready", "dsq_ready", "var_done", "ln_std", "ln_scaled", "chi_ready", "clo_ready"))
        sc_copied, sc_cx, sc_y, shi_ready, slo_ready = (
            sem(n) for n in ("sc_copied", "sc_cx", "sc_y", "shi_ready", "slo_ready"))
        gate_sig, br_done, br_used, mlo_ready = (sem(n) for n in ("gate_sig", "br_done", "br_used", "mlo_ready"))
        kv_copied, xvt_done, xvt_copied, xq_copied = (sem(n) for n in ("kv_copied", "xvt_done", "xvt_copied", "xq_copied"))
        xs_done, xs_neg, xs_exp, xs_norm, xt_done, xt_copied, xo_done, xohi_ready, xolo_ready = (
            sem(n) for n in ("xs_done", "xs_neg", "xs_exp", "xs_norm", "xt_done", "xt_copied", "xo_done", "xohi_ready", "xolo_ready"))
        pq_copied, score_done, score_used, top_ready = (sem(n) for n in ("pq_copied", "score_done", "score_used", "top_ready"))
        pick_diff, pick_exp, pick_ready, selT_done, selT_ready = (
            sem(n) for n in ("pick_diff", "pick_exp", "pick_ready", "selT_done", "selT_ready"))
        rows_ready, rows_free, g_copied = (sem(n) for n in ("rows_ready", "rows_free", "g_copied"))
        g_stored = [sem(f"g_stored{k}") for k in range(2)]
        gelu_ready, w_ready, eh_ready, el_ready, v_done, acc_done = (
            sem(n) for n in ("gelu_ready", "w_ready", "eh_ready", "el_ready", "v_done", "acc_done"))
        early_ready = [sem(f"early_ready{s}") for s in range(2)]
        early_stored = [sem(f"early_stored{s}") for s in range(2)]
        gt_loaded = [sem(f"gt_loaded{k}") for k in range(2)]
        act_loaded = [sem(f"act_loaded{k}") for k in range(2)]
        out_ready, out_stored = sem("out_ready"), sem("out_stored")

        block = ctx.enter_context(nc.Block())
        NORMS = 4 * KC
        ACC = PAIRS * KC
        zps = ps[:, 4:7, :].rearrange("p a b -> p (a b)")

        @block.sync
        def _(sp_):
            eng = sp_
            eng.dma_start(h[:, :, :], xT).then_inc(x_loaded, 16)
            eng.dma_start(const[:, :], const_d).then_inc(const_loaded, 16)

            def feed(s, L, use, row, src, width=1024):
                at = eng.snap(row)
                n = eng.snap(L * SPLITS[s] + use)
                eng.wait_ge(split[s], n)
                eng.dma_start(raw[:, SLOT[s]:SLOT[s] + width], src[at]).then_inc(loaded[s], 16)

            with eng.Fori(0, LAYERS) as L:
                lay = eng.snap(L * 1)
                eng.wait_ge(acc_done, L * ACC + KC)
                eng.dma_start(par[:, :], par_d[lay]).then_inc(par_loaded, 16)
                with eng.Fori(0, FRONT // 4) as i:
                    for s in range(4):
                        feed(s, L, i, L * FRONT + i * 4 + s, front_d)
                with eng.Fori(0, KC) as i:
                    for s in range(3):
                        feed(s, L, i + FRONT // 4, L * GATES + i * 3 + s, gates_d)
                    feed(3, L, i + FRONT // 4, L * KC + i, branch_d, 1536)
                eng.wait_ge(conv_ready, (L + 1) * SB_TILES)
                eng.dma_start(mem[:, :, :], memT).then_inc(mem_loaded, 16)
                XB = (BACK - LISTS) // 4
                with eng.Fori(0, XB) as i:
                    for s in range(4):
                        feed(s, L, i + G1, L * BACK + i * 4 + s, back_d)
                for s in range(4):
                    feed(s, L, G1 + XB, L * BACK + (s + BACK - LISTS), back_d)
                lay = eng.snap(L * 1)
                eng.wait_ge(h_ready, (L + 1) * ROUNDS)
                eng.dma_start(keys[:, :, :], keys_d[lay]).then_inc(keys_loaded, 16)
                with eng.Fori(1, LISTS // 4) as i:
                    for s in range(4):
                        feed(s, L, i + (G1 + XB), L * BACK + i * 4 + (s + BACK - LISTS), back_d)
                for s in range(2):
                    feed(s, L, FIRST, L * STREAM + s, expert_d)

                def early_pair(i, gates=None):
                    for s in range(2):
                        feed(s, L, i + (FIRST + 1), L * STREAM + i * 2 + (2 + s), expert_d)
                    if gates is not None:
                        store_gates(*gates)
                    for s in range(2):
                        at = eng.snap(i * 2 + s)
                        eng.wait_ge(early_ready[s], L * EARLY + i + 1)
                        eng.dma_start(early_d[at], early[:, s, :]).then_inc(early_stored[s], 16)

                def store_gates(b, half, q):
                    at = eng.snap(b * 2 + half)
                    if q == 0:
                        eng.wait_ge(g_copied, (L * TB + b) * (P // 4) + (half + 1) * (HB // 4))
                    eng.dma_start(gate_d[at, :, PARTS[q]:PARTS[q + 1], :], gbuf[:, half, PARTS[q]:PARTS[q + 1], :]).then_inc(g_stored[half], 16)

                with eng.Fori(0, LEAD) as i:
                    early_pair(i)
                with eng.Fori(0, TB) as b:
                    with eng.Fori(0, WITH // 2) as g:
                        early_pair(b * (WITH + BEHIND) + g + LEAD)
                    for half, n in ((0, WITH // 2), (1, BEHIND)):
                        for q in range(n):
                            early_pair(b * (WITH + BEHIND) + (LEAD + WITH // 2 * (half + 1) + q), (b, half, q) if q < PIECES else None)
                for s in range(2):
                    eng.wait_ge(early_stored[s], (L + 1) * (EARLY * 16))
                eng.nop(nofuse=True)
                with eng.Fori(0, LATE - 1) as i:
                    for s in range(2):
                        feed(2 + s, L, i + FIRST, L * STREAM + i * 4 + (2 * EARLY + 2 + s), expert_d)
                    for s in range(2):
                        feed(s, L, i + (FIRST + EARLY + 1), L * STREAM + i * 4 + (2 * EARLY + 4 + s), expert_d)
                for s in range(2):
                    feed(2 + s, L, FIRST + LATE - 1, L * STREAM + (STREAM - 2 + s), expert_d)
            eng.wait_ge(out_ready, KC)
            eng.dma_start(outT, h[:, :, :]).then_inc(out_stored, 16)
            eng.wait_ge(out_stored, 16)

        @block.gpsimd
        def _(pool):
            eng = nc.gpsimd

            def cut(s, L, use, width=1024):
                a, b = SLOT[s], SLOT[s] + width
                pool.wait_ge(loaded[s], (L * SPLITS[s] + use + 1) * 16)
                pool.wait_ge(used[s], L * USED[s] + use)
                pool.nop(nofuse=True)
                eng.tensor_copy(whi[:, a:b], raw[:, a:b])
                pool.drain()
                eng.tensor_tensor(wlo[:, a:b], raw[:, a:b], whi[:, a:b].bitcast(F32), ALU.subtract).then_inc(split[s], 1)

            def low(s, L, count):
                a, b = SLOT[s], SLOT[s] + 1024
                pool.wait_ge(rounded[s], L * ROUNDED[s] + count)
                eng.tensor_tensor(wlo[:, a:b], raw[:, a:b], whi[:, a:b].bitcast(F32), ALU.subtract).then_inc(split[s], 1)

            def lows(L, n, done):
                with pool.Fori(0, n) as i:
                    for s in range(4):
                        low(s, L, i + ((KC - 1 if s < 3 else 0) + done + 1))

            with pool.Fori(0, LAYERS) as L:
                pool.wait_ge(v_done, L * ACC)
                pool.nop(nofuse=True)
                with pool.Fori(0, FRONT // 4) as i:
                    for s in range(4):
                        cut(s, L, i)
                for s in range(3):
                    cut(s, L, FRONT // 4)
                cut(3, L, FRONT // 4, width=1536)
                with pool.Fori(1, KC) as i:
                    for s in range(3):
                        low(s, L, i)
                    cut(3, L, i + FRONT // 4, width=1536)
                with pool.Fori(G1, G1 + 4) as i:
                    for s in range(4):
                        cut(s, L, i)
                lows(L, 5, 0)
                with pool.Fori(G1 + 9, G1 + 11) as i:
                    for s in range(4):
                        cut(s, L, i)
                lows(L, 3, 5)
                with pool.Fori(0, EARLY) as i:
                    for s in range(2):
                        low(s, L, i + (KC - 1 + 8 + 1))
                with pool.Fori(0, LATE) as i:
                    for s in range(4):
                        low(s, L, i + ((KC - 1 if s < 3 else 0) + 8 + 1 + (EARLY if s < 2 else 0)))

        @block.scalar
        def _(act):
            A = nc.scalar.activation
            eps6, eps5 = small[:, 0:1], small[:, 1:2]

            def panel(s, L, use):
                act.wait_ge(used[s], L * USED[s] + use + 1)

            def round_panel(s, L, use):
                act.wait_ge(loaded[s], (L * SPLITS[s] + use + 1) * 16)
                A(whi[:, SLOT[s]:SLOT[s] + 1024], raw[:, SLOT[s]:SLOT[s] + 1024], ACT.Copy).then_inc(rounded[s], 1)

            def norm(L, k, src, w, hi):
                for c in range(KC):
                    n = k * KC + c
                    act.wait_ge(sq_used, L * NORMS + (n - 1 if n >= 2 else 0))
                    A(sq[:, c % 2, 0:w], src(c), ACT.Square).then_inc(sq_ready, 1)
                act.wait_ge(sq_used, L * NORMS + (k + 1) * KC)
                A(std[:, 0:w], ps[:, 7, 0:w], ACT.Sqrt, scale=1.0 / D, bias=eps6).then_inc(std_ready, 1)
                for c in range(KC if hi is not None else 0):
                    act.wait_ge(xf_ready, L * NORMS + k * KC + c + 1)
                    A(hi[:, c, :], xf[:, c % 2, 0:w], ACT.Copy).then_inc(xhi_ready, 1)

            act.wait_ge(consts_ready, 4)
            act.wait_ge(x_loaded, 16)
            with act.Fori(0, LAYERS) as L:
                act.wait_ge(par_loaded, (L + 1) * 16)
                act.wait_ge(acc_done, L * ACC + KC)
                norm(L, 0, lambda c: h[:, c, :], T, xhi)
                for i in range(12):
                    panel(i % 4, L, i // 4)
                    A((qT, kT, vT)[i // 4][:, i % 4, :], ps[:, i % 4, :], ACT.Copy, scale=0.125 if i < 4 else 1.0).then_inc(qkv_copied, 1)
                for b in range(TB):
                    act.wait_ge(vt_done, L * TB + b + 1)
                    A(vtok[:, b, :], ps[:, 4 + b, :], ACT.Copy).then_inc(vt_copied, 1)

                def cv(ct):
                    n = 2 * ct + 1
                    panel(n % 4, L, 3 + n // 4)
                    act.wait_ge(cv_u, L * SB_TILES + max(0, ct - 1))
                    A(xf[:, ct % 2, :], ps[:, n % 4, :], ACT.Sigmoid).then_inc(cv_sig, 1)

                def sc_copy(ct):
                    n = 8 + 3 * ct + 1
                    panel(n % 4, L, 3 + n // 4)
                    act.wait_ge(sc_cx, L * SB_TILES + ct)
                    A(sc_c[:, :], ps[:, n % 4, :], ACT.Copy).then_inc(sc_copied, 1)

                def sc_hi(ct):
                    act.wait_ge(sc_y, L * SB_TILES + ct + 1)
                    A(bhi[:, 8 + ct, :], yt[:, ct % 2, :], ACT.Copy).then_inc(shi_ready, 1)

                for hd in range(SB_HEADS):
                    n = L * SB_HEADS + hd + 1
                    act.wait_ge(z_done, n)
                    A(soft[:, :], zps[:, 0:ZCOLS], ACT.Abs)
                    act.drain()
                    A(soft[:, :], soft[:, :], ACT.Exp, scale=-1.0)
                    act.drain()
                    A(soft[:, :], soft[:, :], ACT.Ln, bias=1.0).then_inc(ln_ready, 1)
                    act.wait_ge(c_done, n)
                    A(soft[:, :], zps[:, 0:ZCOLS], ACT.Exp).then_inc(a_ready, 1)
                    if hd < 4:
                        cv(hd)
                    if hd >= 4 and hd != 5:
                        sc_copy(max(0, hd - 5))
                    if hd >= 6:
                        sc_hi(hd - 6)
                    if hd % 2:
                        act.wait_ge(y_done, n)
                        A(bhi[:, hd // 2, :], ps[:, 7, :], ACT.Copy).then_inc(yhi_ready, 1)
                sc_hi(2)
                sc_copy(3)
                sc_hi(3)
                for ct in range(SB_TILES):
                    act.wait_ge(dev_ready, L * SB_TILES + ct + 1)
                    if ct >= 2:
                        act.wait_ge(var_done, L * SB_TILES + ct - 1)
                    A(sq[:, ct % 2, :], conv[:, ct, :], ACT.Square).then_inc(dsq_ready, 1)
                act.wait_ge(var_done, (L + 1) * SB_TILES)
                A(std[:, :], ps[:, 7, :], ACT.Sqrt, scale=1.0 / (SB_TILES * P), bias=eps5).then_inc(ln_std, 1)
                for ct in range(SB_TILES):
                    act.wait_ge(ln_scaled, L * SB_TILES + ct + 1)
                    A(conv[:, ct, :], conv[:, ct, :], ACT.Silu, scale=pc("lng", ct), bias=pc("lnb", ct))
                    act.drain()
                    A(bhi[:, 4 + ct, :], conv[:, ct, :], ACT.Copy).then_inc(chi_ready, 1)
                for dt in range(KC):
                    act.wait_ge(mlo_ready, L * KC + dt)
                    for b in range(3):
                        panel(b, L, FRONT // 4 + dt)
                        A(sg[:, b, :], ps[:, b, :], ACT.Sigmoid, bias=pc("bg", b * KC + dt)).then_inc(gate_sig, 1)
                        if dt + 1 < KC:
                            round_panel(b, L, FRONT // 4 + dt + 1)
                act.wait_ge(mlo_ready, (L + 1) * KC)
                act.wait_ge(mem_loaded, (L + 1) * 16)
                norm(L, 1, lambda c: mem[:, c, :], N_MEM, mhi)
                act.wait_ge(h_ready, L * ROUNDS + KC)
                norm(L, 2, lambda c: h[:, c, :], T, xhi)
                base = FRONT // 4 + KC + 2
                for i in range(16):
                    panel(i % 4, L, base + i // 4)
                    A((xkT if i < 8 else xvT)[:, i % 8, :], ps[:, i % 8, 0:N_MEM], ACT.Copy).then_inc(kv_copied, 1)
                    if i >= 4:
                        round_panel(i % 4, L, base + i // 4 + 1)
                def xq_copy(i):
                    panel(i % 4, L, base + 4 + i // 4)
                    A(xqT[:, i, :], ps[:, 2 + i % 2, :], ACT.Copy, scale=XA_DH ** -0.5).then_inc(xq_copied, 1)
                    round_panel(i % 4, L, base + 4 + i // 4 + 1)

                def xv_copy():
                    for m in range(MB):
                        act.wait_ge(xvt_done, L * MB + m + 1)
                        A(xv[:, m, :], ps[:, 4 + 2 * m:6 + 2 * m, :].rearrange("p a b -> p (a b)"), ACT.Copy).then_inc(xvt_copied, 1)

                def xs_exps(hd):
                    act.wait_ge(xs_neg, L * XA_HEADS + hd + 1)
                    for tb in range(TB):
                        a = 8 + 4 * (hd % 2) + tb
                        A(prob[:, hd % 2, tb * N_MEM:(tb + 1) * N_MEM],
                          ps[:, tb // 2, (tb % 2) * N_MEM:(tb % 2 + 1) * N_MEM],
                          ACT.Exp, bias=small[:, a:a + 1], accum_out=small[:, a + 8:a + 9]).then_inc(xs_exp, 1)

                def xt_copies(hd):
                    act.wait_ge(xo_done, L * (XA_HEADS * 2) + hd * 2)
                    for m in range(MB):
                        act.wait_ge(xt_done, L * (XA_HEADS * MB) + hd * MB + m + 1)
                        A(probT[:, m, :], ps[:, 4 + m, :], ACT.Copy).then_inc(xt_copied, 1)

                def xo_copies(hd):
                    for c in range(2):
                        act.wait_ge(xo_done, L * (XA_HEADS * 2) + hd * 2 + c + 1)
                        A(ohi[:, 2 * hd + c, :], ps[:, 6 + c, :], ACT.Copy).then_inc(xohi_ready, 1)

                xq_copy(0)
                xq_copy(1)
                xv_copy()
                xs_exps(0)
                xq_copy(2)
                xq_copy(3)
                xt_copies(0)
                xs_exps(1)
                xq_copy(4)
                xo_copies(0)
                xq_copy(5)
                xt_copies(1)
                xs_exps(2)
                xq_copy(6)
                xo_copies(1)
                xq_copy(7)
                xt_copies(2)
                xs_exps(3)
                xo_copies(2)
                xt_copies(3)
                xo_copies(3)
                act.wait_ge(h_ready, (L + 1) * ROUNDS)
                norm(L, 3, lambda c: h[:, c, :], T, xhi)
                for l in range(LISTS):
                    panel(l % 4, L, base + 8 + l // 4)
                    if l >= 2:
                        act.wait_ge(score_done, L * LISTS + l - 1)
                    A(pqT[:, l % 2, :], ps[:, l % 4, :], ACT.Copy).then_inc(pq_copied, 1)
                    if l // 4 < 3 or l % 4 < 2:
                        round_panel(l % 4, L, base + 8 + l // 4 + 1)

                def early_pair(i):
                    for s in range(2):
                        panel(s, L, i + FIRST)
                        act.wait_ge(early_stored[s], (L * EARLY + i) * 16)
                        A(early[:, s, :], ps[:, 5 + s, :], ACT.Gelu).then_inc(early_ready[s], 1)
                        round_panel(s, L, i + (FIRST + 1))

                def pick_weights(b):
                    act.wait_ge(pick_diff, L * TB + b + 1)
                    A(picks[:, :], picks[:, :], ACT.Exp).then_inc(pick_exp, 1)

                def pick_turn(b):
                    act.wait_ge(selT_done, L * TB + b + 1)
                    A(selT[:, :, :].rearrange("p a b -> p (a b)"), ps[:, 4, 0:3 * P], ACT.Copy).then_inc(selT_ready, 1)

                def rows(b):
                    for g in range(WITH):
                        half = g // (WITH // 2)
                        if g % (WITH // 2) == 0:
                            act.wait_ge(g_stored[half], (L * TB + b) * (16 * PIECES))
                        i = b * (WITH + BEHIND) + (LEAD + g)
                        for s in range(2):
                            panel(s, L, i + FIRST)
                            act.wait_ge(early_stored[s], (L * EARLY + i) * 16)
                            A(early[:, s, :], ps[:, 5 + s, :], ACT.Gelu).then_inc(early_ready[s], 1)
                            round_panel(s, L, i + (FIRST + 1))
                            for q in range(4 * g + 2 * s, 4 * g + 2 * s + 2):
                                act.wait_ge(rows_free, (L * TB + b) * P + (4 * q + 4 + HROWS))
                                A(gbuf[:, half, :, 4 * q % HB:4 * q % HB + 4], ps[:, q % 4, :].rearrange("p (t n) -> p n t", t=4), ACT.Copy).then_inc(g_copied, 1)

                for i in range(LEAD):
                    early_pair(L * 0 + i)
                    if i == 2:
                        pick_weights(L * 0)
                pick_turn(L * 0)
                with act.Fori(0, TB - 1) as b:
                    rows(b)
                    for i in range(BEHIND):
                        early_pair(b * (WITH + BEHIND) + (LEAD + WITH + i))
                        if i == 1:
                            pick_weights(b + 1)
                    pick_turn(b + 1)
                rows(L * 0 + (TB - 1))
                for i in range(BEHIND):
                    early_pair(L * 0 + (EARLY - BEHIND + i))

                def sides(j, r):
                    k, r4 = r % 2, r % 4
                    late = r4 == 1
                    first = act.snap(j * 4 + (2 * EARLY + r // 4 * 2) if late else j * 12 + (r // 4 * 6 + (r4 - 1 if r4 else 0) * 2))
                    act.dma_start(gtile[:, k, :, :, :], gate_d[:, :, bass.ds(first, 2), :].rearrange("h p a t -> p h a t")).then_inc(gt_loaded[k], 16)
                    if not late:
                        act.dma_start(act_e[:, k, :, :], early_d[bass.ds(first, 2)].rearrange("a p t -> p a t")).then_inc(act_loaded[k], 16)

                def round_use(j, step):
                    if step >= len(ROUND):
                        j, wrap = j + 1, len(ROUND)
                    else:
                        wrap = 0
                    before = step - 2
                    pair = 2 * (step % 2)
                    if before < 0:
                        act.wait_ge(v_done, (L * PAIRS + j * RV) * KC)
                    elif ROUND[before] == "v":
                        r = ROUND[:before].count("v")
                        act.wait_ge(v_done, (L * PAIRS + (j * RV - (RV if wrap else 0)) + (r + 1)) * KC)
                    for m in range(2):
                        if before >= 0 and ROUND[before] == "u":
                            act.wait_ge(used[pair + m], L * USED[pair + m] + j + (FIRST + 1 + (0 if pair else EARLY)))
                        round_panel(pair + m, L, j * (len(ROUND) // 2) + (FIRST + (0 if pair else EARLY) + (step - wrap) // 2))

                def late_gelu(j, r):
                    act.wait_ge(w_ready, (L * PAIRS + j * RV + (r - 1)) * 2)
                    for m in range(2):
                        s = m if r == 1 else 2 + m
                        act.wait_ge(used[s], L * USED[s] + j + (FIRST + 1 + (EARLY if r == 1 else 0)))
                        A(act_e[:, 1, m, :], ps[:, m, :], ACT.Gelu).then_inc(gelu_ready, 1)

                def high(j, r, more):
                    for m in range(2):
                        act.wait_ge(w_ready, (L * PAIRS + j * RV + r) * 2 + (m + 1))
                        A(eh[:, r % 2, m, :], weighted[:, m, :], ACT.Copy).then_inc(eh_ready, 1)
                    if more:
                        sides(*((j, r + 2) if r + 2 < RV else (j + 1, r + 2 - RV)))

                def expert_round(j, last):
                    r = 0
                    for step, what in enumerate(ROUND):
                        if step and ROUND[step - 1] == "u":
                            late_gelu(j, r + 1)
                        if not (last and step + 1 == len(ROUND)):
                            round_use(j, step + 1)
                        if what == "v":
                            r += 1
                            if r < RV:
                                high(j, r, not last or r + 2 < RV)
                            elif not last:
                                high(j + 1, 0, True)

                for s in range(2):
                    act.wait_ge(g_stored[s], (L + 1) * (TB * 16 * PIECES))
                    act.wait_ge(early_stored[s], (L + 1) * (EARLY * 16))
                act.nop(nofuse=True)
                sides(L * 0, 0)
                sides(L * 0, 1)
                high(L * 0, 0, True)
                with act.Fori(0, NROUNDS - 1) as j:
                    expert_round(j, False)
                expert_round(L * 0 + (NROUNDS - 1), True)
            act.wait_ge(acc_done, LAYERS * ACC + KC)
            norm(LAYERS, 0, lambda c: h[:, c, :], T, None)

        @block.vector
        def _(dve):
            V = nc.vector
            TT, TS, STT = V.tensor_tensor, V.tensor_scalar, V.scalar_tensor_tensor
            drain = dve.drain

            def panel(s, L, use):
                dve.wait_ge(used[s], L * USED[s] + use + 1)

            def hold(s_, n):
                dve.wait_ge(s_, n)
                dve.nop(nofuse=True)

            def norm(L, k, src, w, g, lo, hi):
                dve.wait_ge(std_ready, L * 4 + k + 1)
                V.reciprocal(std[:, 0:w], std[:, 0:w])
                drain()

                def low(c):
                    dve.wait_ge(xhi_ready, L * NORMS + k * KC + c + 1)
                    TT(lo[:, c, :], xf[:, c % 2, 0:w], hi[:, c, :].bitcast(F32), ALU.subtract).then_inc(xlo_ready, 1)

                for c in range(KC):
                    if c >= 2:
                        drain()
                    STT(out=xf[:, c % 2, 0:w], in0=src(c), scalar=pc(g, c), in1=std[:, 0:w], op0=ALU.mult, op1=ALU.mult).then_inc(xf_ready, 1)
                    if c:
                        low(c - 1)
                low(KC - 1)
                drain()

            V.memset(small[:, 0:1], 1e-6).then_inc(consts_ready, 1)
            V.memset(small[:, 1:2], 1e-5).then_inc(consts_ready, 1)
            V.memset(cpad[:, 0:2], 0.0).then_inc(rows_free, HROWS)
            V.memset(upad[:, 0, 0:2], 0.0).then_inc(acc_done, KC)
            dve.wait_ge(const_loaded, 16)
            V.tensor_copy(identb[:, :], cst("ident")).then_inc(consts_ready, 1)
            V.tensor_copy(negmaskb[:, :], cst("negmask")).then_inc(consts_ready, 1)
            dve.wait_ge(x_loaded, 16)
            dve.nop(nofuse=True)
            with dve.Fori(0, LAYERS) as L:
                drain()
                dve.wait_ge(par_loaded, (L + 1) * 16)
                for ct in range(SB_TILES):
                    V.memset(upad[:, ct, 0:CV_TAPS - 1], 0.0)
                V.memset(cpad[:, 0:SC_TAPS - 1], 0.0)
                norm(L, 0, lambda c: h[:, c, :], T, "mix_g", xlo, xhi)

                def cv(ct):
                    dve.wait_ge(cv_sig, L * SB_TILES + ct + 1)
                    TT(upad[:, ct, 30:30 + T], ps[:, (2 * ct) % 4, :], xf[:, ct % 2, :], ALU.mult).then_inc(cv_u, 1)

                def taps(ct, lo, hi):
                    for k in range(lo, hi):
                        drain()
                        w = pc("cw", ct * CV_TAPS + k)
                        if k == 0:
                            ins = TS(conv[:, ct, :], upad[:, ct, 0:T], w, pc("cb", ct), ALU.mult, ALU.add)
                        else:
                            ins = STT(out=conv[:, ct, :], in0=upad[:, ct, k:k + T], scalar=w, in1=conv[:, ct, :], op0=ALU.mult, op1=ALU.add)
                    if hi == CV_TAPS:
                        ins.then_inc(conv_ready, 1)

                def sc(ct):
                    b0, x0 = 8 + 3 * ct, 8 + 3 * ct + 2
                    dve.wait_ge(sc_copied, L * SB_TILES + ct + 1)
                    panel(x0 % 4, L, 3 + x0 // 4)
                    TT(cpad[:, 2:2 + T], ps[:, x0 % 4, :], sc_c[:, :], ALU.mult).then_inc(sc_cx, 1)
                    drain()
                    TS(sc_o[:, :], cpad[:, 0:T], pc("scw", ct * SC_TAPS), None, ALU.mult)
                    for k in range(1, SC_TAPS):
                        drain()
                        STT(out=sc_o[:, :], in0=cpad[:, k:k + T], scalar=pc("scw", ct * SC_TAPS + k), in1=sc_o[:, :], op0=ALU.mult, op1=ALU.add)
                    drain()
                    TT(yt[:, ct % 2, :], ps[:, b0 % 4, :], sc_o[:, :], ALU.mult).then_inc(sc_y, 1)

                def sc_lo(ct):
                    dve.wait_ge(shi_ready, L * SB_TILES + ct + 1)
                    TT(blo[:, 8 + ct, :], yt[:, ct % 2, :], bhi[:, 8 + ct, :].bitcast(F32), ALU.subtract).then_inc(slo_ready, 1)

                for hd in range(SB_HEADS):
                    dve.wait_ge(ln_ready, L * SB_HEADS + hd + 1)
                    STT(out=sp[:, :], in0=zps[:, 0:ZCOLS], scalar=0.0, in1=soft[:, :], op0=ALU.max, op1=ALU.add).then_inc(sp_ready, 1)
                    if hd == 5:
                        sc(0)
                    if hd >= 1:
                        taps((hd - 1) // 2, *((0, 16) if (hd - 1) % 2 == 0 else (16, CV_TAPS)))
                    if hd < 4:
                        cv(hd)
                    if hd >= 6:
                        sc_lo(hd - 6)
                    if hd >= 6:
                        drain()
                        sc(hd - 5)
                    if hd % 2:
                        dve.wait_ge(yhi_ready, L * SB_TILES + hd // 2 + 1)
                        TT(blo[:, hd // 2, :], ps[:, 7, :], bhi[:, hd // 2, :].bitcast(F32), ALU.subtract).then_inc(ylo_ready, 1)
                taps(3, 16, CV_TAPS)
                sc_lo(2)
                drain()
                sc(3)
                sc_lo(3)
                dve.wait_ge(mu_done, L + 1)
                for ct in range(SB_TILES):
                    STT(out=conv[:, ct, :], in0=ps[:, 6, :], scalar=-1.0 / (SB_TILES * P), in1=conv[:, ct, :],
                        op0=ALU.mult, op1=ALU.add).then_inc(dev_ready, 1)
                dve.wait_ge(ln_std, L + 1)
                V.reciprocal(std[:, :], std[:, :])
                drain()
                for ct in range(SB_TILES):
                    TT(conv[:, ct, :], conv[:, ct, :], std[:, :], ALU.mult).then_inc(ln_scaled, 1)
                for ct in range(SB_TILES):
                    dve.wait_ge(chi_ready, L * SB_TILES + ct + 1)
                    TT(blo[:, 4 + ct, :], conv[:, ct, :], bhi[:, 4 + ct, :].bitcast(F32), ALU.subtract).then_inc(clo_ready, 1)
                drain()
                def merge(dt, order, last):
                    for n, b in enumerate(order):
                        dve.wait_ge(gate_sig, (L * KC + dt) * 3 + (b + 1))
                        if b == last:
                            dve.wait_ge(used[3], L * USED[3] + dt + (FRONT // 4 + 1))
                        else:
                            dve.wait_ge(br_done, (L * KC + dt) * 2 + (n + 1))
                        TT(sg[:, b, :], ps[:, 3 + b, :], sg[:, b, :], ALU.mult).then_inc(br_used, 1)
                        if n:
                            drain()
                            TT(sg[:, 0, :], sg[:, 0, :], sg[:, b, :], ALU.add)
                    drain()
                    V.tensor_copy(mghi[:, dt, :], sg[:, 0, :])
                    drain()
                    TT(mglo[:, dt, :], sg[:, 0, :], mghi[:, dt, :].bitcast(F32), ALU.subtract).then_inc(mlo_ready, 1)

                merge(L * 0, (0, 2, 1), 1)
                with dve.Fori(1, KC) as dt:
                    merge(dt, (0, 1, 2), 2)
                drain()

                def residual(use, part=range(KC)):
                    for i in part:
                        panel(i % 4, L, use + i // 4)
                        TT(h[:, i, :], h[:, i, :], ps[:, i % 4, :], ALU.add).then_inc(h_ready, 1)

                residual(G1, range(0, 4))
                drain()
                norm(L, 1, lambda c: mem[:, c, :], N_MEM, "mem_g", mlo, mhi)
                residual(G1, range(4, KC))
                drain()
                norm(L, 2, lambda c: h[:, c, :], T, "xa_g", xlo, xhi)
                def softmax(hd):
                    a = 8 + 4 * (hd % 2)
                    dve.wait_ge(xs_done, L * XA_HEADS + hd + 1)
                    V.tensor_reduce(small[:, a + 16:a + 20], ps[:, 0:2, :].rearrange("p a (b m) -> p (a b) m", b=2), AX.X, ALU.max)
                    drain()
                    TS(small[:, a:a + 4], small[:, a + 16:a + 20], -1.0, None, ALU.mult).then_inc(xs_neg, 1)
                    dve.wait_ge(xs_exp, (L * XA_HEADS + hd + 1) * TB)
                    V.reciprocal(small[:, a + 24:a + 28], small[:, a + 8:a + 12])
                    drain()
                    for tb in range(TB):
                        TS(prob[:, hd % 2, tb * N_MEM:(tb + 1) * N_MEM], prob[:, hd % 2, tb * N_MEM:(tb + 1) * N_MEM],
                           small[:, a + 24 + tb:a + 25 + tb], None, ALU.mult).then_inc(xs_norm, 1)

                for hd in range(XA_HEADS + 1):
                    if hd < XA_HEADS:
                        softmax(hd)
                    if hd:
                        for c in range(2 * hd - 2, 2 * hd):
                            dve.wait_ge(xohi_ready, L * KC + c + 1)
                            TT(olo[:, c, :], ps[:, 6 + c % 2, :], ohi[:, c, :].bitcast(F32), ALU.subtract).then_inc(xolo_ready, 1)
                residual(FRONT // 4 + KC + 8)
                norm(L, 3, lambda c: h[:, c, :], T, "ffn_g", xlo, xhi)
                for l in range(LISTS):
                    hold(score_done, L * LISTS + l + 1)
                    scores = [ps[:, 4 + l % 4, tb * NK:(tb + 1) * NK] for tb in range(TB)]
                    for tb in range(TB):
                        V.max(vals[:, tb, l, 0:8], scores[tb])
                    drain()
                    for tb in range(TB):
                        V.match_replace(rest[:, tb, :], vals[:, tb, l, 0:8], scores[tb], NEG)
                    for tb in range(TB):
                        V.max_index(inds[:, tb, l, 0:8], vals[:, tb, l, 0:8], scores[tb]).then_inc(score_used, 1)
                    drain()
                    for tb in range(TB):
                        V.max(vals[:, tb, l, 8:16], rest[:, tb, :])
                    drain()
                    for tb in range(TB):
                        V.max_index(inds[:, tb, l, 8:16], vals[:, tb, l, 8:16], rest[:, tb, :])
                    drain()
                with dve.Fori(0, TB) as b:
                    v4 = vals[:, b, :, :].rearrange("p (h q) k -> p h q k", q=2)
                    i4 = inds[:, b, :, :].rearrange("p (h q) k -> p h q k", q=2)
                    TT(cand[:, :, :].rearrange("p h (i j) -> p h i j", i=TOPK),
                       v4[:, :, 0, :].unsqueeze(3).to_broadcast([P, PH, TOPK, TOPK]),
                       v4[:, :, 1, :].unsqueeze(2).to_broadcast([P, PH, TOPK, TOPK]), ALU.add)
                    drain()
                    first = [slice(hd * TOPK, hd * TOPK + 8) for hd in range(PH)]
                    second = [slice(hd * TOPK + 8, (hd + 1) * TOPK) for hd in range(PH)]
                    for hd in range(PH):
                        V.max(picks[:, first[hd]], cand[:, hd, :])
                    drain()
                    for hd in range(PH):
                        V.max_index(pick_i[:, first[hd]], picks[:, first[hd]], cand[:, hd, :])
                    drain()
                    for hd in range(PH):
                        V.match_replace(cand[:, hd, :], picks[:, first[hd]], cand[:, hd, :], NEG)
                    drain()
                    for hd in range(PH):
                        V.max(picks[:, second[hd]], cand[:, hd, :])
                    drain()
                    for hd in range(PH):
                        V.max_index(pick_i[:, second[hd]], picks[:, second[hd]], cand[:, hd, :])
                    p3 = picks[:, :].rearrange("p (h k) -> p h k", k=TOPK)
                    V.tensor_copy(small[:, 40:48], p3[:, :, 0])
                    drain()
                    TT(p3, p3, small[:, 40:48].unsqueeze(2).to_broadcast([P, PH, TOPK]), ALU.subtract).then_inc(pick_diff, 1)
                    TS(rank[:, 0, :], pick_i[:, :], 4, None, ALU.logical_shift_right)
                    TS(rank[:, 1, :], pick_i[:, :], TOPK - 1, None, ALU.bitwise_and)
                    l4 = lookup[:, :, :].rearrange("p (h k) j -> p h k j", h=PH)
                    for q in range(2):
                        drain()
                        TT(lookup[:, :, :], rank[:, q, :].unsqueeze(2).to_broadcast([P, SEL, TOPK]),
                           cst("iota16", TOPK).unsqueeze(1).to_broadcast([P, SEL, TOPK]), ALU.is_equal)
                        drain()
                        TT(l4, l4, i4[:, :, q, :].unsqueeze(2).to_broadcast([P, PH, TOPK, TOPK]), ALU.mult)
                        drain()
                        V.tensor_reduce(eidx[:, q, :], lookup[:, :, :], AX.X, ALU.add)
                    dve.wait_ge(pick_exp, L * TB + b + 1)
                    V.tensor_reduce(small[:, 48:56], p3, AX.X, ALU.add)
                    drain()
                    V.reciprocal(small[:, 40:48], small[:, 48:56])
                    drain()
                    TT(eidx[:, 2, :].rearrange("p (h k) -> p h k", k=TOPK), p3,
                       small[:, 40:48].unsqueeze(2).to_broadcast([P, PH, TOPK]), ALU.mult).then_inc(pick_ready, 1)
                    dve.wait_ge(selT_ready, L * TB + b + 1)
                    dve.nop(nofuse=True)
                    with dve.Fori(0, P // HROWS) as g:
                        for k in range(HROWS):
                            t = dve.snap(g * HROWS + k)
                            dve.wait_ge(rows_free, (L * TB + b) * P + g * HROWS + (k + 1))
                            TS(onehot2[:, k, :], cst("iota"), selT[:, 1, bass.ds(t, 1)], None, ALU.is_equal)
                            TS(onehot1[:, k, :], cst("iota"), selT[:, 0, bass.ds(t, 1)], selT[:, 2, bass.ds(t, 1)],
                               ALU.is_equal, ALU.mult).then_inc(rows_ready, 1)

                def by_half(x):
                    return x.rearrange("p (h t) -> p h t", t=HB)

                def weigh(j, r):
                    k, n = r % 2, L * PAIRS + j * RV + r
                    drain()
                    dve.wait_ge(gt_loaded[k], (L * (PAIRS // 2) + j * (RV // 2) + (r // 2 + 1)) * 16)
                    if k == 0:
                        dve.wait_ge(act_loaded[0], (L * (PAIRS // 2) + j * (RV // 2) + (r // 2 + 1)) * 16)
                    elif r % 4 == 3:
                        dve.wait_ge(act_loaded[1], (L * (PAIRS // 4) + j * (RV // 4) + (r // 4 + 1)) * 16)
                    for m in range(2):
                        if r % 4 == 1:
                            dve.wait_ge(gelu_ready, (L * NROUNDS + j) * (2 * RU) + (r // 4 * 2 + m + 1))
                        dve.wait_ge(eh_ready, n * 2)
                        TT(by_half(weighted[:, m, :]), by_half(act_e[:, k, m, :]), gtile[:, k, :, m, :], ALU.mult).then_inc(w_ready, 1)
                    for m in range(2):
                        dve.wait_ge(eh_ready, n * 2 + (m + 1))
                        TT(el[:, k, m, :], weighted[:, m, :], eh[:, k, m, :].bitcast(F32), ALU.subtract).then_inc(el_ready, 1)

                def gather(n, r):
                    for c in range(KC):
                        dve.wait_ge(v_done, (L * PAIRS + n) * KC + (c + 1))
                        TT(h[:, c, :], h[:, c, :], ps[:, down_bank(r, c), :], ALU.add).then_inc(acc_done, 1)

                for s in range(2):
                    hold(g_stored[s], (L + 1) * (TB * 16 * PIECES))
                weigh(L * 0, 0)
                with dve.Fori(0, NROUNDS - 1) as j:
                    for r in range(RV):
                        weigh(*((j, r + 1) if r + 1 < RV else (j + 1, 0)))
                        gather(j * RV + r, r)
                for r in range(RV):
                    if r + 1 < RV:
                        weigh(L * 0 + (NROUNDS - 1), r + 1)
                    gather(L * 0 + (PAIRS - RV + r), r)
            dve.wait_ge(std_ready, LAYERS * 4 + 1)
            V.reciprocal(std[:, :], std[:, :])
            drain()
            for c in range(KC):
                STT(out=h[:, c, :], in0=h[:, c, :], scalar=pc("fin_g", c), in1=std[:, :], op0=ALU.mult, op1=ALU.mult).then_inc(out_ready, 1)

        @block.tensor
        def _(pe):
            MM, TR = nc.tensor.matmul, nc.tensor.transpose

            def linear(s, L, use, out, ahi, alo, chunks=range(KC), w0=0, done=None, part=None, each=None):
                part = part or range(len(chunks))
                if part[0] == 0:
                    pe.wait_ge(split[s], L * SPLITS[s] + use + 1)
                for i in part:
                    c = chunks[i]
                    if each is not None:
                        pe.wait_ge(each[0], each[1] + (i + 1))
                    a = SLOT[s] + (w0 + i) * P
                    for n, (w, x) in enumerate(((whi, ahi), (whi, alo), (wlo, ahi))):
                        ins = MM(out, w[:, a:a + P], x[:, c, :], start=(i == 0 and n == 0), stop=(i == len(chunks) - 1 and n == 2))
                if part[-1] == len(chunks) - 1:
                    ins.then_inc(used[s] if done is None else done, 1)

            def norm(L, k, w):
                for c in range(KC):
                    pe.wait_ge(sq_ready, L * NORMS + k * KC + c + 1)
                    MM(ps[:, 7, 0:w], cst("ones"), sq[:, c % 2, 0:w], start=(c == 0), stop=(c == KC - 1)).then_inc(sq_used, 1)

            pe.wait_ge(consts_ready, 4)
            pe.nop(nofuse=True)
            with pe.Fori(0, LAYERS) as L:
                pe.wait_ge(acc_done, L * ACC + KC)
                norm(L, 0, T)
                for s in range(4):
                    linear(s, L, 0, ps[:, s, :], xhi, xlo, each=None if s else (xlo_ready, L * NORMS))
                with pe.Fori(1, 3) as i:
                    for s in range(4):
                        pe.wait_ge(qkv_copied, L * 12 + i * 4 - (3 - s))
                        linear(s, L, i, ps[:, s, :], xhi, xlo)
                pe.wait_ge(qkv_copied, (L + 1) * 12)
                for b in range(TB):
                    for t in range(SB_TILES):
                        ins = TR(ps[:, 4 + b, t * P:(t + 1) * P], vT[:, t, b * P:(b + 1) * P], cst("ident"))
                    ins.then_inc(vt_done, 1)
                pe.wait_ge(vt_copied, (L + 1) * TB)

                def front(n, part=range(KC)):
                    if part[0]:
                        pass
                    elif 4 <= n < 8:
                        pe.wait_ge(cv_u, L * SB_TILES + n // 2 - 1)
                    elif 8 <= n < 12:
                        pe.wait_ge(cv_u, L * SB_TILES + (4 if n >= 10 else 3))
                    elif n >= 12:
                        tile, which = divmod(n - 12, 3)
                        pe.wait_ge((sc_y, sc_copied, sc_cx)[which], L * SB_TILES + tile + 1)
                    linear(n % 4, L, 3 + n // 4, ps[:, n % 4, :], xhi, xlo, part=part)

                for hd in range(SB_HEADS):
                    r, tile = 64 * (hd % 2), hd // 2
                    pe.wait_ge(a_ready, L * SB_HEADS + hd)
                    for sb in range(TB):
                        z = zps[:, ZO[sb]:ZO[sb] + ZW[sb]]
                        MM(z, kT[r:r + 64, tile, sb * P:(sb + 1) * P], qT[r:r + 64, tile, sb * P:T], start=(sb != 3), stop=False, skip_group_check=True)
                        ins = MM(z[:, 0:P], identb[:, :], negmaskb[:, :], start=False, stop=False, skip_group_check=True)
                    ins.then_inc(z_done, 1)
                    front(2 * hd)
                    front(2 * hd + 1, range(0, 4))
                    pe.wait_ge(sp_ready, L * SB_HEADS + hd + 1)
                    for sb in range(TB - 1, -1, -1):
                        z = zps[:, ZO[sb]:ZO[sb] + ZW[sb]]
                        for sj in range(sb + 1, TB):
                            MM(z[:, ZW[sb] - ZW[sj]:], cst("negones"), sp[:, ZO[sj]:ZO[sj] + ZW[sj]], start=False, stop=False, skip_group_check=True)
                        ins = MM(z, cst("tri"), sp[:, ZO[sb]:ZO[sb] + ZW[sb]], start=False, stop=True, skip_group_check=True)
                    ins.then_inc(c_done, 1)
                    front(2 * hd + 1, range(4, KC))
                    pe.wait_ge(a_ready, L * SB_HEADS + hd + 1)
                    pe.wait_ge(ylo_ready, L * SB_TILES + tile)
                    for sb in range(TB):
                        ins = MM(ps[r:r + 64, 7, sb * P:T], vtok[:, sb, hd * 64:(hd + 1) * 64], soft[:, ZO[sb]:ZO[sb] + ZW[sb]],
                                 start=(sb == 0), stop=(sb == TB - 1), skip_group_check=True)
                    ins.then_inc(y_done, 1)
                for n in range(16, 20):
                    front(n)
                for b in range(3):
                    pe.wait_ge(sc_y, L * SB_TILES + (4 if b else 3))
                    linear(b, L, FRONT // 4, ps[:, b, :], xhi, xlo)
                def branch(dt, b, last=2, each=None):
                    linear(3, L, dt + FRONT // 4, ps[:, 3 + b, :], bhi, blo, range(4 * b, 4 * b + 4), 4 * b, None if b == last else br_done, each=each)

                pe.wait_ge(conv_ready, (L + 1) * SB_TILES)
                for ct in range(SB_TILES):
                    ins = MM(ps[:, 6, :], cst("ones"), conv[:, ct, :], start=(ct == 0), stop=(ct == SB_TILES - 1))
                ins.then_inc(mu_done, 1)
                pe.wait_ge(slo_ready, (L + 1) * SB_TILES)
                branch(L * 0, 0, last=1)
                pe.wait_ge(ylo_ready, (L + 1) * SB_TILES)
                for ct in range(SB_TILES):
                    pe.wait_ge(dsq_ready, L * SB_TILES + ct + 1)
                    MM(ps[:, 7, :], cst("ones"), sq[:, ct % 2, :], start=(ct == 0), stop=(ct == SB_TILES - 1)).then_inc(var_done, 1)
                branch(L * 0, 2, last=1)
                branch(L * 0, 1, last=1, each=(clo_ready, L * SB_TILES))
                with pe.Fori(1, KC) as dt:
                    pe.wait_ge(gate_sig, (L * KC + dt) * 3)
                    for b in range(3):
                        linear(b, L, dt + FRONT // 4, ps[:, b, :], xhi, xlo)
                    pe.wait_ge(br_used, (L * KC + dt) * 3)
                    for b in range(3):
                        branch(dt, b)
                pe.wait_ge(gate_sig, (L + 1) * (KC * 3))
                for i in range(2):
                    for s in range(4):
                        if i:
                            pe.wait_ge(h_ready, L * ROUNDS + s + 1)
                        linear(s, L, G1 + i, ps[:, s, :], mghi, mglo, each=None if s or i else (mlo_ready, L * KC))
                    if i == 0:
                        norm(L, 1, N_MEM)
                for i in range(16):
                    if i == 4:
                        pe.wait_ge(std_ready, L * 4 + 2)
                        norm(L, 2, T)
                    if i < 4:
                        pe.wait_ge(h_ready, L * ROUNDS + 5 + i)
                    if i == 7:
                        pe.wait_ge(std_ready, L * 4 + 3)
                    if i >= 8:
                        pe.wait_ge(kv_copied, L * 16 + i - 7)
                    linear(i % 4, L, G1 + 2 + i // 4, ps[:, i % 8, 0:N_MEM], mhi, mlo, each=None if i else (xlo_ready, L * NORMS + KC))
                pe.wait_ge(kv_copied, (L + 1) * 16)
                pe.wait_ge(xlo_ready, L * NORMS + 3 * KC)

                def xa_query(i):
                    if i >= 2:
                        pe.wait_ge(xq_copied, L * KC + i - 1)
                    linear(i % 4, L, G1 + 6 + i // 4, ps[:, 2 + i % 2, :], xhi, xlo)

                def xa_scores(hd):
                    pe.wait_ge(xs_exp, (L * XA_HEADS + hd) * TB)
                    pe.wait_ge(xq_copied, L * KC + 2 * hd + 2)
                    for tb in range(TB):
                        for c in range(2):
                            ins = MM(ps[:, tb // 2, (tb % 2) * N_MEM:(tb % 2 + 1) * N_MEM],
                                     xqT[:, 2 * hd + c, tb * P:(tb + 1) * P], xkT[:, 2 * hd + c, :], start=(c == 0), stop=(c == 1))
                    ins.then_inc(xs_done, 1)

                def xa_turn(hd):
                    pe.wait_ge(xs_norm, (L * XA_HEADS + hd + 1) * TB)
                    pe.wait_ge(xt_copied, L * (XA_HEADS * MB) + hd * MB)
                    for m in range(MB):
                        for tb in range(TB):
                            a = tb * N_MEM + m * P
                            ins = TR(ps[:, 4 + m, tb * P:(tb + 1) * P], prob[:, hd % 2, a:a + P], cst("ident"))
                        ins.then_inc(xt_done, 1)

                def xa_out(hd):
                    pe.wait_ge(xt_copied, L * (XA_HEADS * MB) + (hd + 1) * MB)
                    pe.wait_ge(xolo_ready, L * KC + 2 * hd)
                    for c in range(2):
                        for m in range(MB):
                            ins = MM(ps[:, 6 + c, :], xv[:, m, (2 * hd + c) * P:(2 * hd + c + 1) * P], probT[:, m, :], start=(m == 0), stop=(m == MB - 1))
                        ins.then_inc(xo_done, 1)

                def wo(s, row, part=range(KC)):
                    linear(s, L, G1 + 8 + row, ps[:, s, :], ohi, olo, part=part)

                xa_query(0)
                xa_query(1)
                for m in range(MB):
                    for c in range(KC):
                        ins = TR(ps[:, 4 + 2 * m + c // 4, (c % 4) * P:(c % 4 + 1) * P], xvT[:, c, m * P:(m + 1) * P], cst("ident"))
                    ins.then_inc(xvt_done, 1)
                xa_scores(0)
                xa_query(2)
                xa_query(3)
                pe.wait_ge(xvt_copied, (L + 1) * MB)
                xa_turn(0)
                xa_scores(1)
                xa_query(4)
                xa_out(0)
                xa_query(5)
                xa_turn(1)
                xa_scores(2)
                xa_query(6)
                xa_out(1)
                xa_query(7)
                xa_turn(2)
                xa_scores(3)
                pe.wait_ge(xq_copied, (L + 1) * KC)
                pe.wait_ge(xolo_ready, L * KC + 4)
                wo(2, 0, range(0, 4))
                xa_out(2)
                wo(3, 0, range(0, 4))
                xa_turn(3)
                pe.wait_ge(xolo_ready, L * KC + 6)
                wo(2, 0, range(4, 6))
                xa_out(3)
                wo(3, 0, range(4, 6))
                pe.wait_ge(xolo_ready, L * KC + 8)
                wo(2, 0, range(6, 8))
                wo(3, 0, range(6, 8))
                for s in range(2):
                    wo(s, 0)
                for s in range(4):
                    pe.wait_ge(h_ready, L * ROUNDS + KC + s + 1)
                    wo(s, 1)
                norm(L, 3, T)
                pe.wait_ge(h_ready, (L + 1) * ROUNDS)
                pe.wait_ge(std_ready, L * 4 + 4)
                pe.wait_ge(keys_loaded, (L + 1) * 16)

                def query(l):
                    if l >= 4:
                        pe.wait_ge(pq_copied, L * LISTS + l - 3)
                    linear(l % 4, L, G1 + 10 + l // 4, ps[:, l % 4, :], xhi, xlo, each=None if l else (xlo_ready, L * NORMS + 3 * KC))

                def score(l):
                    pe.wait_ge(pq_copied, L * LISTS + l + 1)
                    if l >= 4:
                        pe.wait_ge(score_used, (L * LISTS + l - 3) * TB)
                    for tb in range(TB):
                        ins = MM(ps[:, 4 + l % 4, tb * NK:(tb + 1) * NK], pqT[:, l % 2, tb * P:(tb + 1) * P], keys[:, l, :], start=True, stop=True)
                    ins.then_inc(score_done, 1)

                query(0)
                for l in range(1, LISTS):
                    query(l)
                    score(l - 1)
                score(LISTS - 1)
                def early_panel(s, i):
                    pe.wait_ge(early_ready[s], L * EARLY + i)
                    linear(s, L, i + FIRST, ps[:, 5 + s, :], xhi, xlo)

                def turn(b):
                    pe.wait_ge(pick_ready, L * TB + b + 1)
                    for q in range(3):
                        ins = TR(ps[:, 4, q * P:(q + 1) * P], eidx[:, q, :], cst("ident"))
                    ins.then_inc(selT_done, 1)

                pe.wait_ge(score_used, L * (LISTS * TB) + (LISTS - 1) * TB)
                pe.nop(nofuse=True)
                with pe.Fori(0, LEAD) as i:
                    for s in range(2):
                        early_panel(s, i)
                turn(L * 0)

                def rows(b):
                    with pe.Fori(0, WITH) as g:
                        for s in range(2):
                            early_panel(s, b * (WITH + BEHIND) + g + LEAD)
                            for k in range(8 * s, 8 * s + 8):
                                if k % 8 == 0:
                                    pe.wait_ge(g_copied, (L * TB + b) * (P // 4) + g * 4)
                                pe.wait_ge(rows_ready, (L * TB + b) * P + g * 16 + (k + 1))
                                MM(ps[:, k // 4, (k % 4) * NK:(k % 4 + 1) * NK], onehot2[:, k % HROWS, :], onehot1[:, k % HROWS, :],
                                   start=True, stop=True).then_inc(rows_free, 1)
                    for i in range(BEHIND):
                        for s in range(2):
                            early_panel(s, b * (WITH + BEHIND) + (LEAD + WITH + i))

                with pe.Fori(0, TB - 1) as b:
                    rows(b)
                    turn(b + 1)
                rows(L * 0 + (TB - 1))
                pe.wait_ge(g_copied, (L + 1) * (TB * P // 4))
                for s in range(2):
                    pe.wait_ge(early_ready[s], (L + 1) * EARLY)
                pe.nop(nofuse=True)

                def up(j, r, pair, use):
                    pe.wait_ge(gelu_ready, (L * NROUNDS + j) * (2 * RU) + r // 4 * 2)
                    for m in range(2):
                        linear(pair + m, L, use, ps[:, m, :], xhi, xlo)

                def down(j, r, pair, use):
                    n = L * PAIRS + j * RV + r
                    pe.wait_ge(el_ready, n * 2 + 2)
                    for m in range(2):
                        pe.wait_ge(split[pair + m], L * SPLITS[pair] + use + 1)
                    for c in range(KC):
                        if c >= 6:
                            pe.wait_ge(acc_done, n * KC + (c - 5 + KC))
                        elif r % 2:
                            pe.wait_ge(acc_done, n * KC + (c + 3))
                        else:
                            pe.wait_ge(acc_done, n * KC + (c + 5 if c < 4 else c + 1))
                        for m in range(2):
                            a = SLOT[pair + m] + c * P
                            for q, (w, x) in enumerate(((whi, eh), (whi, el), (wlo, eh))):
                                ins = MM(ps[:, down_bank(r, c), :], w[:, a:a + P], x[:, r % 2, m, :], start=(m == 0 and q == 0), stop=(m == 1 and q == 2))
                        ins.then_inc(v_done, 1)

                with pe.Fori(0, NROUNDS) as j:
                    r = 0
                    for step, what in enumerate(ROUND):
                        pair = 2 * (step % 2)
                        use = j * (len(ROUND) // 2) + (FIRST + (0 if pair else EARLY) + step // 2)
                        if what == "u":
                            up(j, r + 1, pair, use)
                        else:
                            down(j, r, pair, use)
                            r += 1
            norm(LAYERS, 0, T)


def kernel(**inputs):
    import numpy as np
    import concourse.bacc as bacc
    from concourse.bass_utils import run_bass_kernel_spmd

    a = {k: np.ascontiguousarray(v) for k, v in inputs.items()}

    def rows(w):
        lead, (K, N) = w.shape[:-2], w.shape[-2:]
        w = w.reshape(*lead, K // P, P, N // P, P)
        n = len(lead)
        return np.ascontiguousarray(w.transpose(*range(n), n + 2, n + 1, n, n + 3)).reshape(*lead, N // P, P, K)

    def cols(v):
        return v.reshape(LAYERS, -1, P).transpose(0, 2, 1)

    w_in = rows(a["w_in"])
    cv, sc, gate = w_in[:, 12:20], w_in[:, 20:32], w_in[:, 32:56]
    cv = cv[:, [0, 4, 1, 5, 2, 6, 3, 7]]
    sc = sc[:, [0, 4, 8, 1, 5, 9, 2, 6, 10, 3, 7, 11]]
    gate = gate[:, [b * KC + dt for dt in range(KC) for b in range(3)]]
    branch = rows(a["w_branch"]).transpose(0, 2, 3, 1, 4)
    par = np.concatenate([
        cols(a["norm_mix_g"]), cols(a["norm_xa_g"]), cols(a["norm_mem_g"]), cols(a["norm_ffn_g"]),
        a["conv_dw_w"].reshape(LAYERS, CV_TAPS, SB_TILES, P).transpose(0, 3, 2, 1).reshape(LAYERS, P, -1),
        cols(a["conv_dw_b"]), cols(a["conv_ln_g"]), cols(a["conv_ln_b"]),
        a["sc_w"].reshape(LAYERS, SC_TAPS, SB_TILES, P).transpose(0, 3, 2, 1).reshape(LAYERS, P, -1),
        cols(a["b_gate"]), np.stack([a["final_g"].reshape(KC, P).T] * LAYERS)], axis=2)
    i = np.arange(P, dtype=np.float32)
    low = (i[:, None] >= i[None, :]).astype(np.float32)
    const = np.concatenate([
        np.eye(P, dtype=np.float32), np.ones((P, P), np.float32), -np.ones((P, P), np.float32),
        -low, np.tile(i, (P, 1)), low * np.float32(-1e30), np.tile(i[:TOPK], (P, 1))], axis=1)
    L = LAYERS
    order = [(0, n) for n in range(2 * EARLY)]
    for j in range(NROUNDS):
        r = 0
        for what in ROUND:
            q = r + (what == "u")
            n = 2 * EARLY + 4 * j + q // 4 * 2 if q % 4 == 1 else 12 * j + q // 4 * 6 + max(0, q % 4 - 1) * 2
            order += [(int(what == "v"), n), (int(what == "v"), n + 1)]
            r += what == "v"
    u_v = rows(a["peer_u"].transpose(0, 2, 1)), a["peer_v"].reshape(L, NK, P, D)
    experts = np.stack([u_v[which][:, n] for which, n in order], axis=1)
    data = {
        "xT": a["x"][0].T.reshape(KC, P, T).transpose(1, 0, 2),
        "memT": a["mem"][0].T.reshape(KC, P, N_MEM).transpose(1, 0, 2),
        "par": par,
        "const": const,
        "front": np.concatenate([w_in[:, 0:12], cv, sc], axis=1).reshape(L * FRONT, P, D),
        "gates": gate.reshape(L * GATES, P, D),
        "branch": branch.reshape(L * KC, P, 12 * P),
        "back": np.concatenate([rows(a[n]) for n in ("w_out", "xa_wkv", "xa_wq", "xa_wo", "peer_wq")], axis=1).reshape(L * BACK, P, D),
        "keys": a["peer_keys"].reshape(L, LISTS, NK, P).transpose(0, 3, 1, 2),
        "experts": experts.reshape(L * STREAM, P, D),
    }
    nc = bacc.Bacc("TRN2", target_bir_lowering=False, num_devices=1)
    arrays, args = {}, []
    for name, v in data.items():
        v = np.ascontiguousarray(v)
        arrays[f"in_{name}"] = v
        args.append(nc.dram_tensor(f"in_{name}", v.shape, mybir.dt.from_np(v.dtype), kind="ExternalInput").ap())
    out = nc.dram_tensor("out", (P, KC, T), F32, kind="ExternalOutput").ap()
    build_trunk(nc, *args, out)
    r = run_bass_kernel_spmd(nc, [arrays], core_ids=[0])
    return r.results[0]["out"].transpose(2, 1, 0).reshape(1, T, D)
```
